# Optimizing a Trainium2 kernel written in Bass

```python
import jax, jax.numpy as jnp
from jax import lax
import numpy as np

D_MODEL = 1024
BATCH = 1
SEQ = 512
DEPTH = 2

N_MIXERS = 2
N_CONV_LAYERS = (DEPTH + 1) // 2
N_SGU_LAYERS = DEPTH // 2
CONV_WIDTH = 3
SGU_WIDTH = 2 * D_MODEL
SGU_HEADS = 8
SGU_HEAD_DIM = SGU_WIDTH // SGU_HEADS
CHUNK = 128
N_EXPERTS = 16
N_GROUPS = 4
EXPERTS_PER_GROUP = N_EXPERTS // N_GROUPS
TOP_K = 2
EXPERT_FF = D_MODEL // 2
DEEPNORM_ALPHA = (2 * DEPTH) ** 0.25
DEEPNORM_BETA = (8 * DEPTH) ** -0.25
LN_EPS = 1e-5

kernel_name = 'hybrid_conv_sgu_grouped_moe_deepnorm'

def layer_norm(x, g, b):
    xf = x.astype(jnp.float32)
    mu = jnp.mean(xf, axis=-1, keepdims=True)
    var = jnp.mean(jnp.square(xf - mu), axis=-1, keepdims=True)
    y = (xf - mu) * lax.rsqrt(var + LN_EPS)
    return (y * g.astype(jnp.float32) + b.astype(jnp.float32)).astype(x.dtype)

def short_conv_mixer(x, w_in, conv_w, w_out):
    d = x.shape[-1]
    bch = jnp.einsum('bsd,de->bse', x, w_in)
    b_gate, c_gate, h = jnp.split(bch, 3, axis=-1)
    z = lax.conv_general_dilated(
        c_gate * h, conv_w[:, None, :], window_strides=(1,),
        padding=[(CONV_WIDTH - 1, 0)],
        dimension_numbers=('NWC', 'WIO', 'NWC'), feature_group_count=d)
    return jnp.einsum('bsd,de->bse', b_gate * z, w_out)

def chunked_sgu_mixer(x, w_in, ln_g, ln_b, w_s, b_s, w_out):
    bn, s, _ = x.shape
    uv = jax.nn.gelu(jnp.einsum('bsd,de->bse', x, w_in), approximate=False)
    u, v = jnp.split(uv, 2, axis=-1)
    v = layer_norm(v, ln_g, ln_b)
    v = v.reshape(bn, s // CHUNK, CHUNK, SGU_HEADS, SGU_HEAD_DIM)
    causal = jnp.tril(jnp.ones((CHUNK, CHUNK), dtype=bool))
    w_causal = jnp.where(causal[None], w_s, 0)
    mixed = jnp.einsum('hij,bnjhc->bnihc', w_causal, v) + b_s.T[:, :, None]
    mixed = mixed.reshape(bn, s, SGU_WIDTH)
    return jnp.einsum('bsf,fd->bsd', u * mixed, w_out)

def grouped_moe(x, router_w, router_bias, w_gate, w_up, w_down):
    bn, s, d = x.shape
    xt = x.reshape(bn * s, d)
    logits = jnp.einsum('td,de->te', xt.astype(jnp.float32), router_w.astype(jnp.float32))
    scores = jax.nn.sigmoid(logits)
    biased = (scores + router_bias.astype(jnp.float32)).reshape(-1, N_GROUPS, EXPERTS_PER_GROUP)
    group_score = lax.top_k(biased, TOP_K)[0].sum(-1)
    group = jnp.argmax(group_score, axis=-1)
    in_group = jnp.take_along_axis(biased, group[:, None, None], axis=1)[:, 0]
    _, local_idx = lax.top_k(in_group, TOP_K)
    expert_idx = group[:, None] * EXPERTS_PER_GROUP + local_idx
    w = jnp.take_along_axis(scores, expert_idx, axis=1)
    w = w / jnp.sum(w, axis=-1, keepdims=True)
    gates = jnp.einsum('tk,tke->te', w, jax.nn.one_hot(expert_idx, N_EXPERTS, dtype=jnp.float32)).astype(x.dtype)
    y = jnp.zeros_like(xt)
    for e in range(N_EXPERTS):
        h = jax.nn.silu(xt @ w_gate[e]) * (xt @ w_up[e])
        y = y + gates[:, e:e + 1] * (h @ w_down[e])
    return y.reshape(bn, s, d)

def setup_inputs(seed: int = 0) -> dict:
    key = jax.random.key(seed)
    ks = jax.random.split(key, 20)
    f32 = jnp.float32
    D, E, F = D_MODEL, N_EXPERTS, EXPERT_FF
    nrm = lambda k, shape, scale: jax.random.normal(k, shape, f32) * scale
    return {
        'x': nrm(ks[0], (BATCH, SEQ, D), 1.0),
        'a_w_in': nrm(ks[1], (N_CONV_LAYERS, D, 3 * D), D ** -0.5),
        'a_conv_w': nrm(ks[2], (N_CONV_LAYERS, CONV_WIDTH, D), CONV_WIDTH ** -0.5),
        'a_w_out': nrm(ks[3], (N_CONV_LAYERS, D, D), D ** -0.5 * DEEPNORM_BETA),
        'b_w_in': nrm(ks[4], (N_SGU_LAYERS, D, 2 * SGU_WIDTH), D ** -0.5),
        'b_ln_g': 1.0 + nrm(ks[5], (N_SGU_LAYERS, SGU_WIDTH), 0.02),
        'b_ln_b': nrm(ks[6], (N_SGU_LAYERS, SGU_WIDTH), 0.02),
        'b_ws': nrm(ks[7], (N_SGU_LAYERS, SGU_HEADS, CHUNK, CHUNK), CHUNK ** -0.5),
        'b_bs': 1.0 + nrm(ks[8], (N_SGU_LAYERS, SGU_HEADS, CHUNK), 0.1),
        'b_w_out': nrm(ks[9], (N_SGU_LAYERS, SGU_WIDTH, D), SGU_WIDTH ** -0.5 * DEEPNORM_BETA),
        'router_w': nrm(ks[10], (D, E), D ** -0.5),
        'router_bias': nrm(ks[11], (E,), 0.01),
        'moe_w_gate': nrm(ks[12], (DEPTH, E, D, F), D ** -0.5),
        'moe_w_up': nrm(ks[13], (DEPTH, E, D, F), D ** -0.5),
        'moe_w_down': nrm(ks[14], (DEPTH, E, F, D), F ** -0.5 * DEEPNORM_BETA),
        'ln_mix_g': 1.0 + nrm(ks[15], (DEPTH, D), 0.02),
        'ln_mix_b': nrm(ks[16], (DEPTH, D), 0.02),
        'ln_ffn_g': 1.0 + nrm(ks[17], (DEPTH, D), 0.02),
        'ln_ffn_b': nrm(ks[18], (DEPTH, D), 0.02),
    }

def reference(x, a_w_in, a_conv_w, a_w_out, b_w_in, b_ln_g, b_ln_b, b_ws, b_bs, b_w_out,
              router_w, router_bias, moe_w_gate, moe_w_up, moe_w_down,
              ln_mix_g, ln_mix_b, ln_ffn_g, ln_ffn_b):
    for i in range(DEPTH):
        j = i // N_MIXERS
        if i % N_MIXERS == 0:
            m = short_conv_mixer(x, a_w_in[j], a_conv_w[j], a_w_out[j])
        else:
            m = chunked_sgu_mixer(x, b_w_in[j], b_ln_g[j], b_ln_b[j], b_ws[j], b_bs[j], b_w_out[j])
        x = layer_norm(DEEPNORM_ALPHA * x + m, ln_mix_g[i], ln_mix_b[i])
        f = grouped_moe(x, router_w, router_bias, moe_w_gate[i], moe_w_up[i], moe_w_down[i])
        x = layer_norm(DEEPNORM_ALPHA * x + f, ln_ffn_g[i], ln_ffn_b[i])
    return x


_drawn_inputs = setup_inputs


def setup_inputs(seed=0):
    import zlib

    import numpy as np

    out = dict(_drawn_inputs(seed))
    spreads = {}
    factors = {'b_ln_g': 3.956, 'b_ln_b': 5.588}
    for name, (base, spread) in spreads.items():
        noise = np.random.default_rng([zlib.crc32(name.encode()), seed]).standard_normal(out[name].shape)
        drawn = base * np.exp(spread * noise) if base else spread * noise
        out[name] = __import__('jax').numpy.asarray(drawn.astype(out[name].dtype))
    for name, factor in factors.items():
        out[name] = (out[name] * factor).astype(out[name].dtype)
    return out
```

```python
import concourse.bass as bass
from concourse import mybir
from contextlib import ExitStack

F32 = mybir.dt.float32
F32R = mybir.dt.float32r
BF16 = mybir.dt.bfloat16
I32 = mybir.dt.int32
ALU = mybir.AluOpType
ACT = mybir.ActivationFunctionType
AX = mybir.AxisListType

P = 128
D = 1024
S = 512
NT = S // P
KD = D // P
BANK = 512
E = 16
G = 4
F = 512
KF = F // P
SGU = 2048
NC = SGU // P
H = 8
ALPHA = 4.0 ** 0.25
EPS = 1e-5
KB = 1024

UN = 1024
RING = 8
N_CONV = 3 * KD
CRING = 6
OUT0 = N_CONV
GU, DN = KD, KF
EU = GU + DN
MOE = [OUT0 + KD, 0]
U0 = MOE[0] + E * EU
V0 = U0 + NC
SO0 = V0 + 16
MOE[1] = SO0 + 16
UNITS = MOE[1] + E * EU


def gu0(layer, e):
    return MOE[layer] + (0 if e == 0 else GU + EU * (e - 1))


def dn0(layer, e):
    return MOE[layer] + (GU + EU * e + GU if e < E - 1 else GU + EU * e)


def slot_of(n):
    return n % CRING if n < N_CONV else (n + CRING - N_CONV % RING) % RING


def before(n):
    back = CRING if n < N_CONV else RING
    m = n - back
    return m if m >= 0 and slot_of(m) == slot_of(n) else None


def pool_owned():
    own = [False] * UNITS
    for layer in (0, 1):
        for k in (1, 3, 5, 7):
            own[gu0(layer, 0) + k] = True
        for e in range(1, E):
            own[gu0(layer, e) + 3] = True
        for e in range(E):
            own[dn0(layer, e) + 3] = True
    return own


POOL = pool_owned()
LO_DVE = [sum(not x for x in POOL[:n + 1]) for n in range(UNITS)]
LO_POOL = [sum(POOL[:n + 1]) for n in range(UNITS)]
INDEX = list(range(UNITS))


def pair_count():
    seen, out = [0] * (RING // 2), []
    for n in range(0, UNITS, 2):
        seen[slot_of(n) // 2] += 1
        out += [seen[slot_of(n) // 2]] * 2
    return out


PAIRS = pair_count()


def at(count, n, step, i):
    if isinstance(i, int):
        return count[n + step * i]
    return i * (count[n + step] - count[n]) + count[n]


class Chain:

    def __init__(self, eng, sem):
        self.eng, self.sem, self.n, self.i, self.per = eng, sem, 0, 0, 0

    def post(self, ins):
        ins.then_inc(self.sem, 1)
        self.n += 1

    def sync(self):
        self.eng.wait_ge(self.sem, self.n if isinstance(self.i, int) else self.i * self.per + self.n)

    def step(self, ins):
        self.post(ins)
        self.sync()

    def enter(self, i, per):
        self.i, self.per, self.start = i, per, self.n

    def leave(self, turns):
        assert self.n - self.start == self.per, (self.n - self.start, self.per)
        self.i, self.n = 0, self.start + self.per * turns


def plus(c, i, k=2):
    return k * i + c if isinstance(i, int) else i * k + c


def is_zero(n):
    return isinstance(n, int) and n == 0


def hybrid_decoder(nc, x, x_t, w_dense0, w_moe, w_dense1, conv_w, router_w, router_bias,
                   w_s, b_s, v_gain, v_bias, ln_par, out):
    ctx = ExitStack()
    with ctx:
        base = -(-nc.sbuf_base // 64) * 64
        top = [base]

        def place(name, shape, dt, offset=None):
            size = 2 if dt == BF16 else 4
            for d in shape[1:]:
                size *= d
            if offset is None:
                offset = top[0]
                top[0] += -(-size // 32) * 32
                assert top[0] <= nc.sbuf_usable_end, (name, top[0], nc.sbuf_usable_end)
            else:
                assert offset + size <= 96 * KB, name
                offset += zone
            return nc.alloc_sbuf_tensor_at(name, shape, dt, offset=offset)

        raw = place("raw", [P, RING, UN], F32)
        hi = place("hi", [P, RING, UN], F32R)
        lo = place("lo", [P, RING, UN], F32R)
        zone = top[0]
        top[0] += 96 * KB

        X = place("X", [P, NT, D], F32, 80 * KB)
        xT_hi = place("xT_hi", [P, KD, S], F32R, 0)
        xT_lo = place("xT_lo", [P, KD, S], F32R, 16 * KB)
        xT_raw = place("xT_raw", [P, KD, S], F32, 32 * KB)
        bz_hi = place("bz_hi", [P, KD, S], F32R, 32 * KB)
        bz_lo = place("bz_lo", [P, KD, S], F32R, 48 * KB)
        cgate = place("cgate", [P, S], F32, 64 * KB)
        ch = place("ch", [P, 2 + S], F32, 66 * KB)
        z = place("z", [P, S], F32, 69 * KB)
        U = place("U", [P, NC, S], F32, 32 * KB)
        V = place("V", [P, NC, NT, P], F32, 64 * KB)
        g2_hi = place("g2_hi", [P, NC // 2, S], F32R, 32 * KB)
        g2_lo = place("g2_lo", [P, NC // 2, S], F32R, 64 * KB)
        xTt = [place(f"xTt{l}", [P, KD, P], F32, o) for l, o in ((0, 0), (1, 56 * KB))]
        hot = [place(f"hot{l}", [P, E, P], BF16, o) for l, o in ((0, 4 * KB), (1, 60 * KB))]
        mix_par = [place(f"mix_par{l}", [P, 2, D], F32, o) for l, o in ((0, 72 * KB), (1, 48 * KB))]
        ffn_par = place("ffn_par", [P, 2, D], F32, 72 * KB)
        xg = place("xg", [P, 2, D], F32, 8 * KB)
        xgT_hi = place("xgT_hi", [P, KD, P], F32R, 16 * KB)
        xgT_lo = place("xgT_lo", [P, KD, P], F32R, 20 * KB)
        sgate = place("sgate", [P, F], F32, 24 * KB)
        hid = place("hid", [P, F], F32, 26 * KB)
        hT_hi = place("hT_hi", [P, KF, P], F32R, 28 * KB)
        hT_lo = place("hT_lo", [P, KF, P], F32R, 30 * KB)
        y = place("y", [P, 2, D], F32, 32 * KB)
        yg = place("yg", [P, NT, 2, D], F32, 40 * KB)

        w_over = place("w_over", [P, 2, 2 * UN], F32, 40 * KB)
        y_over = place("y_over", [P, D], F32, 56 * KB)
        x_over = place("x_over", [P, KD, P], F32, 64 * KB)
        h_over = place("h_over", [P, KF, P], F32, 68 * KB)

        ident = place("ident", [P, P], F32)
        ones_f = place("ones_f", [P, P], F32, 68 * KB + 256)
        ones_b = place("ones_b", [P, P], BF16)
        tri = place("tri", [P, P], BF16)
        iota_s = place("iota_s", [P, P], BF16)
        tok_id = place("tok_id", [P, NT, 2], BF16)
        earlier = place("earlier", [P, G, G], F32)
        row0 = place("row0", [P, E], F32)
        eps = place("eps", [P, 1], F32)
        warm = place("warm", [P, 1], F32)
        rw = place("rw", [P, KD, E], F32)
        rbias = place("rbias", [P, E], F32)
        cw = place("cw", [P, KD, 3], F32)
        wcT_at = top[0]
        wcT = place("wcT", [P, H, P], F32)
        ws_sum = place("ws_sum", [P, H, P], F32)
        bsb = place("bsb", [P, H, P], F32)
        vg = place("vg", [P, NC], F32)
        vb = place("vb", [P, NC], F32)
        stats = place("stats", [P, 2, 6], F32)
        mv = place("mv", [P, NT, 2], F32)
        std = place("std", [P, NT], F32)
        rstd = place("rstd", [P, NT], F32)
        nmr = place("nmr", [P, NT], F32)
        score_at = top[0]
        score = place("score", [P, NT, E], F32)
        order = place("order", [P, NT, E], F32)
        rank1 = nc.alloc_sbuf_tensor_at("rank1", [P, P], F32, offset=score_at)
        v_parts = nc.alloc_sbuf_tensor_at("v_parts", [P, NT, 4, 6], F32, offset=score_at)
        most = place("most", [P, 2], I32)
        sel = place("sel", [P, NT, E], BF16)
        posm = place("posm", [P, NT, E], F32)
        idx = place("idx", [P, E], I32)
        idx_col = place("idx_col", [P, 2], I32)
        gate = place("gate", [P, NT, 2], F32)
        rows = place("rows", [P, NT, 2], I32)

        iota_i = place("iota_i", [P, P], I32, 71 * KB + 256)
        def scratch(layer):
            at_ = 70 * KB if layer == 0 else wcT_at - zone
            out = {}
            for name, shape, dt in (
                    ("sig", [E, P], F32),
                    ("biased", [P, E], F32),
                    ("beats", [P, G, G, 2, G], F32),
                    ("rank", [P, E], F32),
                    ("top2", [P, E], F32),
                    ("gsc", [P, G], F32),
                    ("gbeats", [P, G, 2, G], F32),
                    ("grank", [P, G], F32),
                    ("idsf", [P, E], F32),
                    ("most_f", [P, 1], F32),
                    ("gsum", [P, NT], F32),
                    ("rows_f", [P, NT, 2], F32),
                    ("place_", [P, NT, E], F32)):
                size = 4
                for d in shape[1:]:
                    size *= d
                tensor = nc.alloc_sbuf_tensor_at(f"{name}{layer}", shape, dt, offset=zone + at_)
                at_ += -(-size // 32) * 32
                out[name] = tensor
            return out

        scr = [scratch(0), scratch(1)]
        pick = [place(f"pick{l}", [P, NT, 2, E], F32, o) for l, o in ((0, 0), (1, 56 * KB))]
        prod = [place(f"prod{l}", [P, NT, 2, E], F32, o) for l, o in ((0, 1 * KB), (1, 57 * KB))]
        past = [place(f"past{l}", [P, NT, E], F32, o) for l, o in ((0, 2 * KB), (1, 58 * KB))]

        ps = ctx.enter_context(nc.psum_tensor("ps", [P, 8, BANK], F32))
        x_rows = nc.dram_tensor("x_rows", [S, D], F32)
        x_mid = nc.dram_tensor("x_mid", [S, D], F32)
        y_rows = nc.dram_tensor("y_rows", [NT, E, P, D], F32)

        def sem(name):
            return ctx.enter_context(nc.semaphore(name))

        raw_in = [sem(f"raw_in{s}") for s in range(RING // 2)]
        hi_ready = sem("hi_ready")
        lo_ready = sem("lo_ready")
        lo_ready_p = sem("lo_ready_p")
        unit_used = sem("unit_used")
        xt_in = [sem(f"xt_in{c}") for c in range(4)]
        x_in = sem("x_in")
        small_in = sem("small_in")
        ws_in = sem("ws_in")
        par_in = sem("par_in")
        consts = sem("consts")
        dve_step = sem("dve_step")
        pool_step = sem("pool_step")
        act_step = sem("act_step")
        xt_hi = sem("xt_hi")
        xt_lo = sem("xt_lo")
        ws_masked = sem("ws_masked")
        ws_tr = sem("ws_tr")
        ws_copied = sem("ws_copied")
        ws_summed = sem("ws_summed")
        c_ready = sem("c_ready")
        bz_ready = sem("bz_ready")
        bz_hi_ready = sem("bz_hi_ready")
        bz_lo_ready = sem("bz_lo_ready")
        mix_ready = sem("mix_ready")
        mix_taken = sem("mix_taken")
        var_ready = sem("var_ready")
        std_ready = sem("std_ready")
        normed = sem("normed")
        tr_ready = sem("tr_ready")
        tr_taken = sem("tr_taken")
        logit_ready = sem("logit_ready")
        sig_ready = sem("sig_ready")
        s_ready = sem("s_ready")
        sel_ready = sem("sel_ready")
        pos_ready = sem("pos_ready")
        hot_ready = sem("hot_ready")
        ids_ready = sem("ids_ready")
        idx_ready = sem("idx_ready")
        xrow_out = sem("xrow_out")
        xmid_out = sem("xmid_out")
        out_done = sem("out_done")
        xg_in = [sem(f"xg_in{b}") for b in range(2)]
        xgT_ready = sem("xgT_ready")
        xgT_hi_ready = sem("xgT_hi_ready")
        xgT_lo_ready = sem("xgT_lo_ready")
        silu_ready = sem("silu_ready")
        hid_ready = sem("hid_ready")
        hT_ready = sem("hT_ready")
        hT_hi_ready = sem("hT_hi_ready")
        hT_lo_ready = sem("hT_lo_ready")
        y_copied = sem("y_copied")
        y_out = [sem(f"y_out{b}") for b in range(2)]
        gates_done = sem("gates_done")
        yg_in = [sem(f"yg_in{t}") for t in range(NT)]
        yg_scaled = sem("yg_scaled")
        u_copied = sem("u_copied")
        v_ready = sem("v_ready")
        v_copied = sem("v_copied")
        v_stats = sem("v_stats")
        v_root = sem("v_root")
        g_ready = sem("g_ready")
        bs_in = sem("bs_in")
        cnt_ready = sem("cnt_ready")
        most_ready = sem("most_ready")
        v_normed = sem("v_normed")
        v_normed_a = sem("v_normed_a")
        sg_ready = sem("sg_ready")
        sg_taken = sem("sg_taken")
        g_hi_ready = sem("g_hi_ready")
        g_lo_ready = sem("g_lo_ready")
        nh0_taken = sem("nh0_taken")
        x_back = sem("x_back")

        block = ctx.enter_context(nc.Block())

        def lo_sem(n):
            return lo_ready_p if POOL[n] else lo_ready

        def wait_lo(eng, n, step=0, i=0):
            eng.wait_ge(lo_sem(n), at(LO_POOL if POOL[n] else LO_DVE, n, step, i))

        def lo_count(eng, n, step, i, reg):
            value = at(LO_POOL if POOL[n] else LO_DVE, n, step, i)
            if isinstance(value, int):
                return value
            eng.reg_mov(reg, value)
            return reg

        def split_hi(act, n, step=0, i=0):
            s = slot_of(n)
            if n % 2 == 0:
                act.wait_ge(raw_in[s // 2], at(PAIRS, n, step, i) * 16)
            if before(n) is not None:
                act.wait_ge(unit_used, at(INDEX, before(n), step, i) + 1)
            nc.scalar.activation(hi[:, s, :], raw[:, s, :], ACT.Copy).then_inc(hi_ready, 1)

        def split_lo(eng, n, step=0, i=0, count=None):
            s = slot_of(n)
            eng.wait_ge(hi_ready, at(INDEX, n, step, i) + 1 if count is None else count)
            eng.tensor_tensor(lo[:, s, :], raw[:, s, :], hi[:, s, :], ALU.subtract) \
               .then_inc(lo_ready_p if POOL[n] else lo_ready, 1)

        def passes(out_, a_hi, a_lo, b_hi, b_lo, first, last):
            nc.tensor.matmul(out_, a_hi, b_hi, start=first, stop=False)
            nc.tensor.matmul(out_, a_hi, b_lo, start=False, stop=False)
            return nc.tensor.matmul(out_, a_lo, b_hi, start=False, stop=last)

        TRB = (2, 0)
        LGB = (4, 2)
        logit_bank = lambda layer, t: LGB[layer] if t < NT - 1 else 6
        IDB = (5, 3)

        TR_MIX, TR_FFN = (0, 4 * NT), 2 * NT


        def tile_of(t, j):
            return t[:, j, :] if isinstance(j, int) else t[:, bass.ds(j, 1), :].rearrange("p a s -> p (a s)")

        def gated(j):
            if j < NC // 2:
                return xT_hi[:, j, :], xT_lo[:, j, :]
            return g2_hi[:, j - NC // 2, :], g2_lo[:, j - NC // 2, :]

        def slots_hot(eng, layer, pos, t):
            return eng.tensor_tensor(hot[layer][:, :, :], iota_s[:, None, :].to_broadcast([P, E, P]),
                                     pos[:, t, :, None].to_broadcast([P, E, P]), ALU.is_equal)

        class Over:

            def __init__(self, layer):
                def s(name):
                    return sem(f"over{layer}_{name}")
                self.dve, self.pool = s("dve"), s("pool")
                self.hot, self.ids, self.idx = s("hot"), s("ids"), s("idx")
                self.xg, self.tr, self.xo = s("xg"), s("tr"), s("xo")
                self.w, self.used = [s("w0"), s("w1")], s("used")
                self.silu, self.hid, self.hT, self.hTo = s("silu"), s("hid"), s("hT"), s("hTo")
                self.yo, self.out = s("yo"), s("out")

        over = [Over(0), Over(1)]
        EP = EU // 2

        def heavy(eng, layer):
            eng.wait_ge(most_ready, layer + 1)
            return eng.value_load(most[0:1, layer:layer + 1], min_val=0, max_val=S)

        def overflow_pool(pool, layer, spare):
            o, load = over[layer], heavy(pool, layer)
            chain = Chain(pool, o.pool)

            def expert(turn, e):
                q = e + E * (turn - 1)
                if not is_zero(q):
                    pool.wait_ge(o.out, q * 16)
                src = idx[:, e:e + 1] if isinstance(e, int) else idx[:, bass.ds(e, 1)]
                chain.step(nc.gpsimd.tensor_copy(idx_col[:, 0:1], src))
                used = q * EP
                if not isinstance(e, int):
                    pool.reg_mov(spare, used)
                    used = spare
                pool.wait_ge(xrow_out, 16 * NT * (layer + 1))
                pool.indirect_dma_start(
                    out=xg[:, 0, :], out_offset=None, in_=x_rows[:, :],
                    in_offset=bass.IndirectOffsetOnAxis(ap=idx_col[:, 0:1], axis=0)).then_inc(o.xg, 16)
                for k in range(EP):
                    if k >= 2:
                        pool.wait_ge(o.used, q * EP + (k - 1))
                    elif not is_zero(q):
                        pool.wait_ge(o.used, used)
                    pool.dma_start(w_over[:, k % 2, :], w_moe[layer, e, k, :, :]).then_inc(o.w[k % 2], 16)
                pool.wait_ge(o.yo, q + 1)
                pool.dma_start(y_rows[turn, e, :, :], y_over[:, :]).then_inc(o.out, 16)

            for turn in range(1, NT):
                with pool.If(load > P * turn):
                    pool.wait_ge(xgT_ready, E * (layer + 1))
                    pool.wait_ge(o.idx, turn)
                    expert(turn, 0)
                    with pool.Fori(0, E - 1) as i:
                        chain.enter(i, 1)
                        expert(turn, i + 1)
                    chain.leave(E - 1)
                    pool.wait_ge(o.out, 16 * E * turn)
            return load

        def overflow_dve(dve, layer):
            o, load = over[layer], heavy(dve, layer)
            chain = Chain(dve, o.dve)
            for turn in range(1, NT):
                q0 = E * (turn - 1)
                with dve.If(load > P * turn):
                    dve.wait_ge(hT_lo_ready, E * (layer + 1))
                    dve.wait_ge(gates_done, layer + 1)
                    chain.step(nc.vector.tensor_scalar(scr[layer]["place_"][:, :, :], posm[:, :, :], float(P * turn), None,
                                                       ALU.subtract))
                    for t in range(NT):
                        if t:
                            dve.wait_ge(o.ids, NT * (turn - 1) + t)
                        slots_hot(dve, layer, scr[layer]["place_"], t).then_inc(o.hot, 1)
                    dve.wait_ge(o.ids, NT * turn)
                    ids = ps[:, 7, 0:2 * E].rearrange("p (e a) -> p e a", a=2)
                    chain.step(nc.vector.tensor_copy(scr[layer]["idsf"][:, :], ids[:, :, 0]))
                    dve.wait_ge(xgT_ready, E * (layer + 1))
                    nc.vector.tensor_tensor(idx[:, :], scr[layer]["idsf"][:, :], ids[:, :, 1], ALU.add).then_inc(o.idx, 1)
                    with dve.Fori(0, E) as e:
                        dve.wait_ge(o.silu, e + (q0 + 1))
                        nc.vector.tensor_tensor(hid[:, :], sgate[:, :], ps[:, 1, :], ALU.mult).then_inc(o.hid, 1)
                    dve.wait_ge(o.yo, q0 + E)

        def overflow_act(act, layer):
            o, load = over[layer], heavy(act, layer)

            def expert(turn, e):
                q = e + E * (turn - 1)
                act.wait_ge(o.tr, q + 1)
                nc.scalar.activation(x_over[:, :, :].rearrange("p k s -> p (k s)"),
                                     ps[:, 5:7, :].rearrange("p b n -> p (b n)"), ACT.Copy).then_inc(o.xo, 1)
                act.wait_ge(o.used, q * EP + GU // 2)
                nc.scalar.activation(sgate[:, :], ps[:, 0, :], ACT.Silu).then_inc(o.silu, 1)
                act.wait_ge(o.hT, q + 1)
                nc.scalar.activation(h_over[:, :, :].rearrange("p k s -> p (k s)"), ps[:, 4, :], ACT.Copy) \
                         .then_inc(o.hTo, 1)
                act.wait_ge(o.used, q * EP + EP)
                if not is_zero(q):
                    act.wait_ge(o.out, q * 16)
                nc.scalar.activation(y_over[:, :], ps[:, 2:4, :].rearrange("p b n -> p (b n)"), ACT.Copy) \
                         .then_inc(o.yo, 1)

            for turn in range(1, NT):
                with act.If(load > P * turn):
                    expert(turn, 0)
                    with act.Fori(0, E - 1) as i:
                        expert(turn, i + 1)

        def overflow_pe(pe, layer, ids_of):
            o, load = over[layer], heavy(pe, layer)

            def expert(turn, e):
                q = e + E * (turn - 1)
                pe.wait_ge(o.xg, q * 16 + 16)
                for k in range(KD):
                    ins = nc.tensor.transpose(ps[:, 5 + k // 4, (k % 4) * P:(k % 4 + 1) * P],
                                              xg[:, 0, k * P:(k + 1) * P], ident[:, :])
                ins.then_inc(o.tr, 1)
                pe.wait_ge(o.xo, q + 1)
                for k in range(EP):
                    if k == GU // 2:
                        pe.wait_ge(o.hid, q + 1)
                        for f in range(KF):
                            ins = nc.tensor.transpose(ps[:, 4, f * P:(f + 1) * P], hid[:, f * P:(f + 1) * P],
                                                      ident[:, :])
                        ins.then_inc(o.hT, 1)
                        pe.wait_ge(o.hTo, q + 1)
                        if not is_zero(q):
                            pe.wait_ge(o.yo, q)
                    pe.wait_ge(o.w[k % 2], q * (16 * EP // 2) + 16 * (k // 2 + 1))
                    for u in range(2):
                        r = 2 * k + u
                        for h in range(2):
                            cols = slice(u * UN + h * BANK, u * UN + (h + 1) * BANK)
                            if r < GU:
                                ins = nc.tensor.matmul(ps[:, h, :], x_over[:, r, :], w_over[:, k % 2, cols],
                                                       start=(r == 0), stop=(r == GU - 1))
                            else:
                                ins = nc.tensor.matmul(ps[:, 2 + h, :], h_over[:, r - GU, :], w_over[:, k % 2, cols],
                                                       start=(r == GU), stop=(r == EU - 1))
                    ins.then_inc(o.used, 1)

            for turn in range(1, NT):
                with pe.If(load > P * turn):
                    for t in range(NT):
                        pe.wait_ge(o.hot, NT * (turn - 1) + t + 1)
                        ids_of(hot[layer], 7, t).then_inc(o.ids, 1)
                    pe.wait_ge(y_copied, E * (layer + 1))
                    pe.wait_ge(hT_lo_ready, E * (layer + 1))
                    expert(turn, 0)
                    with pe.Fori(0, E - 1) as i:
                        expert(turn, i + 1)

        @block.sync
        def _(sp):
            counts = [sp.alloc_register("count0"), sp.alloc_register("count1")]

            def pair_of(w, c, i, k=2):
                j = plus(c, i, k)
                return w[j if isinstance(j, int) else sp.snap(j)]

            def load_pair(n, src, step=0, i=0):
                s = slot_of(n)
                if before(n) is not None:
                    m = before(n)
                    if POOL[m] != POOL[m + 1]:
                        first = lo_count(sp, m, step, i, counts[0])
                        second = lo_count(sp, m + 1, step, i, counts[1])
                        sp.wait_ge(lo_sem(m), first)
                        sp.wait_ge(lo_sem(m + 1), second)
                    else:
                        wait_lo(sp, m + 1, step, i)
                sp.dma_start(raw[:, s:s + 2, :].rearrange("p u n -> p (u n)"), src).then_inc(raw_in[s // 2], 16)

            def store_y(layer, c, i=0):
                e = plus(c, i)
                sp.wait_ge(y_copied, e + (1 + E * layer))
                sp.dma_start(y_rows[0, e, :, :], y[:, c % 2, :]).then_inc(y_out[c % 2], 16)

            for c in range(4):
                sp.dma_start(xT_raw[:, 2 * c:2 * c + 2, :].rearrange("p k s -> p (k s)"), x_t[c, :, :]) \
                  .then_inc(xt_in[c], 16)
            for m in range(3):
                load_pair(2 * m, w_dense0[m, :, :])
            sp.dma_start(X[:, :, :], x.rearrange("(t p) d -> p t d", p=P)).then_inc(x_in, 16)
            with sp.Fori(0, 3) as i:
                for m in range(3):
                    load_pair(CRING + 2 * m, pair_of(w_dense0, 3 + m, i, 3), CRING, i)
            for m in range(12, 16):
                load_pair(2 * m, w_dense0[m, :, :])

            def experts(layer):
                def expert_pair(c, i, k):
                    e = plus(c, i)
                    return w_moe[layer, e if isinstance(e, int) else sp.snap(e), k, :, :]

                def turn(e, i=0, stores=True):
                    step = 0 if isinstance(i, int) else 2 * EU
                    for k in range(GU // 2):
                        load_pair(gu0(layer, e + 1) + 2 * k, expert_pair(e + 1, i, k), step, i)
                    if stores:
                        store_y(layer, e - 2, i)
                    for k in range(DN // 2):
                        load_pair(dn0(layer, e) + 2 * k, expert_pair(e, i, GU // 2 + k), step, i)

                for k in range(GU // 2):
                    load_pair(gu0(layer, 0) + 2 * k, w_moe[layer, 0, k, :, :])
                turn(0, stores=False)
                turn(1, stores=False)
                with sp.Fori(0, 6) as i:
                    turn(2, i)
                    turn(3, i)
                turn(14)
                for k in range(DN // 2):
                    load_pair(dn0(layer, E - 1) + 2 * k, w_moe[layer, E - 1, GU // 2 + k, :, :])
                for k in range(4):
                    if layer == 0:
                        load_pair(U0 + 2 * k, w_dense1[k, :, :])
                    if k:
                        store_y(layer, E - 4 + k)

            experts(0)
            with sp.Fori(0, 5) as i:
                for m in range(4):
                    load_pair(U0 + 8 + 2 * m, pair_of(w_dense1, 4 + m, i, 4), RING, i)
            experts(1)

        @block.gpsimd
        def _(pool):
            chain = Chain(pool, pool_step)
            spare = pool.alloc_register("spare")
            for t_, v_ in ((eps, EPS), (ones_b, 1.0), (ones_f, 1.0), (warm, 1.0)):
                chain.post(nc.gpsimd.memset(t_[:, :], v_))
            chain.step(nc.gpsimd.memset(ch[:, 0:2], 0.0))
            chain.post(nc.gpsimd.affine_select(out=ident[:, :], in_=ones_f[:, :], compare_op=ALU.is_equal, fill=0.0,
                                               base=0, pattern=[[-1, P]], channel_multiplier=1))
            chain.post(nc.gpsimd.affine_select(out=tri[:, :], in_=ones_b[:, :], compare_op=ALU.is_ge, fill=0.0,
                                               base=0, pattern=[[1, P]], channel_multiplier=-1))
            chain.post(nc.gpsimd.affine_select(out=earlier[:, :, :],
                                               in_=ones_f[:, 0:G * G].rearrange("p (i j) -> p i j", i=G),
                                               compare_op=ALU.is_gt, fill=0.0,
                                               base=0, pattern=[[1, G], [-1, G]], channel_multiplier=0))
            chain.step(nc.gpsimd.iota(iota_i[:, :], pattern=[[1, P]], base=1, channel_multiplier=0))
            chain.step(nc.gpsimd.tensor_copy(iota_s[:, :], iota_i[:, :]))
            chain.step(nc.gpsimd.iota(iota_i[:, 0:E], pattern=[[P, E]], base=-1, channel_multiplier=0))
            chain.step(nc.gpsimd.tensor_copy(row0[:, :], iota_i[:, 0:E]))
            chain.step(nc.gpsimd.iota(iota_i[:, 0:NT], pattern=[[P, NT]], base=0, channel_multiplier=0))
            chain.step(nc.gpsimd.tensor_copy(tok_id[:, :, 0], iota_i[:, 0:NT]))
            chain.step(nc.gpsimd.iota(iota_i[:, 0:NT], pattern=[[0, NT]], base=0, channel_multiplier=1))
            nc.gpsimd.tensor_copy(tok_id[:, :, 1], iota_i[:, 0:NT]).then_inc(consts, 1)
            pool.wait_ge(ws_in, 16)
            nc.gpsimd.affine_select(out=bsb[:, :, :], in_=ws_sum[:, :, :], compare_op=ALU.is_ge, fill=0.0,
                                    base=0, pattern=[[0, H], [-1, P]], channel_multiplier=1).then_inc(ws_masked, 1)
            pool.wait_ge(ws_tr, 1)
            pool.dma_start(bsb[:, :, :].rearrange("p h i -> p (h i)"), b_s.partition_broadcast(P)).then_inc(bs_in, 16)

            def fetch(layer, c, i=0, later=None):
                e, b, n = plus(c, i), c % 2, plus(c + E * layer, i)
                if c + E * layer >= 2:
                    pool.wait_ge(xgT_ready, n - 1)
                    pool.wait_ge(xg_in[b], plus(16 * ((c + E * layer) // 2), i, 16))
                src = idx[:, e:e + 1] if isinstance(e, int) else idx[:, bass.ds(e, 1)]
                chain.step(nc.gpsimd.tensor_copy(idx_col[:, b:b + 1], src))
                if later is not None:
                    pool.reg_mov(spare, later)
                pool.wait_ge(xrow_out, 16 * NT * (layer + 1))
                pool.indirect_dma_start(
                    out=xg[:, b, :], out_offset=None, in_=x_rows[:, :],
                    in_offset=bass.IndirectOffsetOnAxis(ap=idx_col[:, b:b + 1], axis=0)).then_inc(xg_in[b], 16)

            def experts(layer):
                for k in range(GU):
                    if POOL[gu0(layer, 0) + k]:
                        split_lo(pool, gu0(layer, 0) + k)
                pool.wait_ge(idx_ready, layer + 1)
                for e in range(3):
                    fetch(layer, e)

                def turn(e, i=0, fetches=True):
                    step = 0 if isinstance(i, int) else 2 * EU
                    n = gu0(layer, e + 1) + 3
                    if isinstance(i, int):
                        if fetches:
                            fetch(layer, e + 3)
                        split_lo(pool, n)
                    else:
                        fetch(layer, e + 3, i, later=at(INDEX, n, step, i) + 1)
                        split_lo(pool, n, step, i, count=spare)
                    split_lo(pool, dn0(layer, e) + 3, step, i)

                with pool.Fori(0, 6) as i:
                    chain.enter(i, 2)
                    turn(0, i)
                    turn(1, i)
                chain.leave(6)
                turn(12)
                turn(13, fetches=False)
                turn(14, fetches=False)
                split_lo(pool, dn0(layer, E - 1) + 3)

            def combine(layer, load):
                pool.wait_ge(gates_done, layer + 1)
                for b in range(2):
                    pool.wait_ge(y_out[b], 16 * 8 * (layer + 1))
                for turn in range(NT):
                    filled = y_rows.ap()[0:turn + 1].rearrange("t e s d -> (t e s) d")
                    with pool.If(load <= P * (turn + 1)):
                        with pool.If(load > P * turn):
                            for t in range(NT):
                                for k in range(2):
                                    pool.indirect_dma_start(
                                        out=yg[:, t, k, :], out_offset=None, in_=filled,
                                        in_offset=bass.IndirectOffsetOnAxis(ap=rows[:, t, k:k + 1], axis=0)) \
                                        .then_inc(yg_in[t], 16)

            for layer in (0, 1):
                experts(layer)
                load = overflow_pool(pool, layer, spare)
                combine(layer, load)

        @block.scalar
        def _(act):
            preloads = Chain(act, act_step)

            def copy(o, i_):
                return nc.scalar.activation(o, i_, ACT.Copy)

            def preload(func):
                preloads.step(nc.scalar.activation(warm[:, :], eps[:, :], func))

            act.dma_start(ws_sum[:, :, :], w_s).then_inc(ws_in, 16)
            for o, i_ in ((rw[:, :, :], router_w), (rbias[:, :], router_bias.partition_broadcast(P)),
                          (cw[:, :, :], conv_w), (vg[:, :], v_gain), (vb[:, :], v_bias)):
                act.dma_start(o, i_).then_inc(small_in, 16)
            for c in range(4):
                act.wait_ge(xt_in[c], 16)
                copy(xT_hi[:, 2 * c:2 * c + 2, :], xT_raw[:, 2 * c:2 * c + 2, :]).then_inc(xt_hi, 1)
                if c == 0:
                    split_hi(act, 0)
            for n in range(1, CRING):
                split_hi(act, n)
            act.wait_ge(ws_tr, 1)
            copy(wcT[:, :, :].rearrange("p h i -> p (h i)"),
                 ps[:, 0:2, :].rearrange("p b n -> p (b n)")).then_inc(ws_copied, 1)
            act.wait_ge(ws_summed, 1)
            copy(ws_sum[:, :, :].rearrange("p h i -> p (h i)"),
                 ps[:, 2:4, :].rearrange("p b n -> p (b n)")).then_inc(ws_copied, 1)

            def conv_tile(c, i, ahead):
                j = plus(c, i)
                for n in ahead[:-1]:
                    split_hi(act, n, CRING, i)
                act.wait_ge(unit_used, plus(3 * c + 3, i, 6))
                if c:
                    act.wait_ge(bz_ready, j)
                copy(cgate[:, :], ps[:, 3 * (c % 2) + 1, :]).then_inc(c_ready, 1)
                split_hi(act, ahead[-1], CRING, i)
                act.wait_ge(bz_ready, j + 1)
                copy(tile_of(bz_hi, j), z[:, :]).then_inc(bz_hi_ready, 1)

            conv_tile(0, 0, (6, 7, 8))
            conv_tile(1, 0, (9, 10, 11))
            with act.Fori(0, 2) as i:
                conv_tile(2, i, (12, 13, 14))
                conv_tile(3, i, (15, 16, 17))
            conv_tile(6, 0, (24, 25, 26, 27, 28))
            conv_tile(7, 0, (29, 30, 31))

            def params(layer, which, dst):
                for k in range(2):
                    act.dma_start(dst[:, k, :], ln_par[layer, which, k, :].partition_broadcast(P)).then_inc(par_in, 16)

            def root(q, t):
                act.wait_ge(var_ready, q + 1)
                nc.scalar.activation(std[:, t:t + 1], mv[:, t, 1:2], ACT.Sqrt, bias=eps[:, :]).then_inc(std_ready, 1)

            def router_in(layer, t):
                act.wait_ge(normed, 8 * layer + t + 1)
                act.dma_start(x_rows[t * P:(t + 1) * P, :], X[:, t, :]).then_inc(xrow_out, 16)
                for h in range(2):
                    act.wait_ge(tr_ready, TR_MIX[layer] + 2 * t + h + 1)
                    if h == 0 and t:
                        act.wait_ge(logit_ready, NT * layer + t)
                    copy(xTt[layer][:, 4 * h:4 * h + 4, :],
                         ps[:, TRB[layer] + h, :].rearrange("p (k s) -> p k s", k=4)).then_inc(tr_taken, 1)

            def scores(layer, t):
                preload(ACT.Sigmoid)
                act.wait_ge(logit_ready, NT * layer + t + 1)
                nc.scalar.activation(scr[layer]["sig"][:, :], ps[0:E, logit_bank(layer, t), 0:P], ACT.Sigmoid).then_inc(sig_ready, 1)

            def norm_and_route(layer):
                preload(ACT.Sqrt)
                root(8 * layer, 0)
                root(8 * layer + 1, 1)
                for t in range(NT):
                    router_in(layer, t)
                    scores(layer, t)
                    if t < 2:
                        preload(ACT.Sqrt)
                        root(8 * layer + t + 2, t + 2)
                    if t == 2:
                        for k in range(GU):
                            split_hi(act, gu0(layer, 0) + k)

            def experts(layer):
                m0 = E * layer

                def x_hi(c, i=0):
                    act.wait_ge(xgT_ready, plus(c + m0 + 1, i))
                    copy(xgT_hi[:, :, :].rearrange("p k s -> p (k s)"),
                         ps[:, 5:7, :].rearrange("p b n -> p (b n)")).then_inc(xgT_hi_ready, 1)

                def silu(c, step=0, i=0):
                    act.wait_ge(unit_used, at(INDEX, gu0(layer, c) + GU - 1, step, i) + 1)
                    if c + m0:
                        act.wait_ge(hid_ready, plus(c + m0, i))
                    nc.scalar.activation(sgate[:, :], ps[:, 0, :], ACT.Silu).then_inc(silu_ready, 1)

                def h_hi(c, i=0):
                    act.wait_ge(hT_ready, plus(c + m0 + 1, i))
                    copy(hT_hi[:, :, :].rearrange("p k s -> p (k s)"), ps[:, 4, :]).then_inc(hT_hi_ready, 1)

                def y_copy(c, step=0, i=0):
                    act.wait_ge(unit_used, at(INDEX, dn0(layer, c) + DN - 1, step, i) + 1)
                    if c + m0 >= 2:
                        act.wait_ge(y_out[c % 2], plus(16 * ((c + m0) // 2), i, 16))
                    copy(y[:, c % 2, :], ps[:, 2:4, :].rearrange("p b n -> p (b n)")).then_inc(y_copied, 1)

                def turn(e, i=0, more_x=True):
                    step = 0 if isinstance(i, int) else 2 * EU
                    n0 = gu0(layer, e + 1) + GU
                    for k in range(GU - 1):
                        split_hi(act, n0 + k, step, i)
                    silu(e + 1, step, i)
                    if more_x:
                        x_hi(e + 2, i)
                    for k in range(GU - 1, EU):
                        if n0 + k < UNITS:
                            split_hi(act, n0 + k, step, i)
                    y_copy(e, step, i)
                    h_hi(e + 1, i)

                preload(ACT.Silu)
                x_hi(0)
                for k in range(GU - 1):
                    split_hi(act, gu0(layer, 1) + k)
                silu(0)
                x_hi(1)
                split_hi(act, gu0(layer, 1) + GU - 1)
                h_hi(0)
                turn(0)
                turn(1)
                with act.Fori(0, 6) as i:
                    turn(2, i)
                    turn(3, i)
                turn(14, more_x=False)
                y_copy(15)
                if layer == 0:
                    for k in range(4):
                        split_hi(act, U0 + 4 + k)

            def finish(layer, t):
                act.wait_ge(normed, 8 * layer + 4 + t + 1)
                if layer == 1:
                    act.dma_start(out[t * P:(t + 1) * P, :], X[:, t, :]).then_inc(out_done, 16)
                    return
                act.dma_start(x_mid[t * P:(t + 1) * P, :], X[:, t, :]).then_inc(xmid_out, 16)
                for h in range(2):
                    act.wait_ge(tr_ready, TR_FFN + 2 * t + h + 1)
                    copy(xT_hi[:, 4 * h:4 * h + 4, t * P:(t + 1) * P],
                         ps[:, TRB[0] + h, :].rearrange("p (k s) -> p k s", k=4)).then_inc(xt_hi, 1)

            def combine(layer):
                preload(ACT.Sqrt)
                for t in range(NT):
                    act.wait_ge(yg_in[t], 32 * (layer + 1))
                    nc.scalar.activation(yg[:, t, 0, :], yg[:, t, 0, :], ACT.Copy,
                                         scale=gate[:, t, 0:1]).then_inc(yg_scaled, 1)
                    if t:
                        finish(layer, t - 1)
                    root(8 * layer + 4 + t, t)
                finish(layer, NT - 1)

            params(0, 0, mix_par[0])
            norm_and_route(0)
            params(0, 1, ffn_par)
            experts(0)
            overflow_act(act, 0)
            combine(0)

            nc.scalar.activation(warm[:, :], eps[:, :], ACT.Gelu).then_inc(u_copied, 1)
            with act.Fori(0, 2) as i:
                for a in range(8):
                    act.wait_ge(unit_used, plus(U0 + a + 1, i, 8))
                    nc.scalar.activation(tile_of(U, plus(a, i, 8)), ps[:, a % 2, :], ACT.Gelu).then_inc(u_copied, 1)
                    split_hi(act, U0 + 8 + a, RING, i)
            act.wait_ge(xmid_out, 16 * NT)
            for nb in range(4):
                for t in range(NT):
                    if t < NT - 1:
                        act.wait_ge(v_ready, (NT - 1) * nb + t + 1)
                    else:
                        act.wait_ge(unit_used, V0 + 4 * nb + 4)
                    nc.scalar.activation(V[:, 4 * nb:4 * nb + 4, t, :],
                                         ps[:, (nb % 2) * 4 + t, :].rearrange("p (j c) -> p j c", j=4),
                                         ACT.Gelu).then_inc(v_copied, 1)
                for k in range(4):
                    split_hi(act, V0 + 8 + 4 * nb + k)
            preload(ACT.Sqrt)
            act.wait_ge(v_stats, 1)
            nc.scalar.activation(std[:, :], mv[:, :, 1], ACT.Sqrt, bias=eps[:, :]).then_inc(v_root, 1)
            act.wait_ge(v_stats, 2)
            for t in (2, 3):
                nc.scalar.activation(V[:, :, t, :], V[:, :, t, :], ACT.Identity, scale=rstd[:, t:t + 1],
                                     bias=nmr[:, t:t + 1]).then_inc(v_normed_a, 1)
            for j in range(NC):
                act.wait_ge(g_ready, j + 1)
                copy(gated(j)[0], U[:, j, :]).then_inc(g_hi_ready, 1)
                if j >= 3 and j % 2:
                    split_hi(act, SO0 + 8 + (j - 3) // 2)
            act.dma_start(X[:, :, :], x_mid.ap().rearrange("(t p) d -> p t d", p=P)).then_inc(x_back, 16)
            act.wait_ge(g_lo_ready, NC)
            params(1, 0, mix_par[1])
            split_hi(act, SO0 + 15)

            norm_and_route(1)
            params(1, 1, ffn_par)
            experts(1)
            overflow_act(act, 1)
            combine(1)
            act.wait_ge(out_done, 16 * NT)

        @block.vector
        def _(dve):
            chain = Chain(dve, dve_step)

            def own_lo(n, step=0, i=0):
                if not POOL[n]:
                    split_lo(dve, n, step, i)

            for c in range(4):
                dve.wait_ge(xt_hi, c + 1)
                nc.vector.tensor_tensor(xT_lo[:, 2 * c:2 * c + 2, :], xT_raw[:, 2 * c:2 * c + 2, :],
                                        xT_hi[:, 2 * c:2 * c + 2, :], ALU.subtract).then_inc(xt_lo, 1)
                if c == 0:
                    own_lo(0)
            for n in range(1, CRING):
                own_lo(n)
            dve.wait_ge(small_in, 16 * 5)
            dve.wait_ge(consts, 1)
            dve.wait_ge(xt_lo, 4)

            def conv_tile(c, i, ahead):
                j = plus(c, i)
                for n in ahead[:-1]:
                    own_lo(n, CRING, i)
                dve.wait_ge(c_ready, j + 1)
                if c:
                    dve.wait_ge(bz_lo_ready, j)
                bank = 3 * (c % 2)
                chain.step(nc.vector.tensor_tensor(ch[:, 2:2 + S], cgate[:, :], ps[:, bank + 2, :], ALU.mult))
                tap = lambda k: cw[:, j:j + 1, k] if isinstance(j, int) else cw[:, bass.ds(j, 1), k]
                chain.step(nc.vector.tensor_scalar(z[:, :], ch[:, 2:2 + S], tap(2), None, ALU.mult))
                for k in (1, 0):
                    chain.step(nc.vector.scalar_tensor_tensor(out=z[:, :], in0=ch[:, k:k + S], scalar=tap(k),
                                                              in1=z[:, :], op0=ALU.mult, op1=ALU.add))
                nc.vector.tensor_tensor(z[:, :], z[:, :], ps[:, bank, :], ALU.mult).then_inc(bz_ready, 1)
                own_lo(ahead[-1], CRING, i)
                dve.wait_ge(bz_hi_ready, j + 1)
                nc.vector.tensor_tensor(tile_of(bz_lo, j), z[:, :], tile_of(bz_hi, j), ALU.subtract) \
                         .then_inc(bz_lo_ready, 1)

            conv_tile(0, 0, (6, 7, 8))
            conv_tile(1, 0, (9, 10, 11))
            with dve.Fori(0, 2) as i:
                chain.enter(i, 8)
                conv_tile(2, i, (12, 13, 14))
                conv_tile(3, i, (15, 16, 17))
            chain.leave(2)
            conv_tile(6, 0, (24, 25, 26, 27, 28))
            conv_tile(7, 0, (29, 30, 31))

            def norm(q, t, par, n_par):
                for h in range(2):
                    chain.post(nc.vector.bn_stats(stats[:, h, :], X[:, t, h * BANK:(h + 1) * BANK]))
                chain.sync()
                nc.vector.bn_aggr(mv[:, t, :], stats[:, :, :].rearrange("p a b -> p (a b)")).then_inc(var_ready, 1)
                dve.wait_ge(var_ready, q + 1)
                dve.wait_ge(par_in, 32 * n_par)
                chain.step(nc.vector.scalar_tensor_tensor(out=X[:, t, :], in0=X[:, t, :], scalar=mv[:, t, 0:1],
                                                          in1=par[:, 0, :], op0=ALU.subtract, op1=ALU.mult))
                dve.wait_ge(std_ready, q + 1)
                chain.step(nc.vector.reciprocal(rstd[:, t:t + 1], std[:, t:t + 1]))
                nc.vector.scalar_tensor_tensor(out=X[:, t, :], in0=X[:, t, :], scalar=rstd[:, t:t + 1],
                                               in1=par[:, 1, :], op0=ALU.mult, op1=ALU.add).then_inc(normed, 1)

            def mix_norm(layer, t):
                if t < NT - 1:
                    dve.wait_ge(mix_ready, (NT - 1) * layer + t + 1)
                else:
                    dve.wait_ge(unit_used, gu0(layer, 0))
                if layer == 0:
                    dve.wait_ge(x_in, 16)
                    b = (6, 0)[t % 2]
                    cols, src = slice(0, D), ps[:, b:b + 2, :].rearrange("p b n -> p (b n)")
                else:
                    cols, src = slice(BANK, D), ps[:, 4 + t, :]
                nc.vector.scalar_tensor_tensor(out=X[:, t, cols], in0=X[:, t, cols], scalar=ALPHA, in1=src,
                                               op0=ALU.mult, op1=ALU.add).then_inc(mix_taken, 1)
                dve.wait_ge(mix_taken, NT * layer + t + 1)
                norm(8 * layer + t, t, mix_par[layer], 1 + 2 * layer)

            def route(layer, t):
                dve.wait_ge(s_ready, NT * layer + t + 1)
                src = ps[:, LGB[layer], P:P + E]
                chain.post(nc.vector.tensor_copy(score[:, t, :], src))
                chain.step(nc.vector.tensor_tensor(scr[layer]["biased"][:, :], src, rbias[:, :], ALU.add))
                by_g = scr[layer]["biased"][:, :].rearrange("p (g i) -> p g i", g=G)
                other = by_g[:, :, None, :].to_broadcast([P, G, G, G])
                mine = by_g[:, :, :, None].to_broadcast([P, G, G, G])
                chain.post(nc.vector.tensor_tensor(scr[layer]["beats"][:, :, :, 0, :], other, mine, ALU.is_gt))
                chain.step(nc.vector.tensor_tensor(scr[layer]["beats"][:, :, :, 1, :], other, mine, ALU.is_equal))
                chain.step(nc.vector.tensor_tensor(scr[layer]["beats"][:, :, :, 1, :], scr[layer]["beats"][:, :, :, 1, :],
                                                   earlier[:, None, :, :].to_broadcast([P, G, G, G]), ALU.mult))
                chain.step(nc.vector.reduce_sum(scr[layer]["rank"][:, :], scr[layer]["beats"][:, :, :, :, :].rearrange("p g i a j -> p (g i) (a j)"),
                                                axis=AX.X))
                chain.step(nc.vector.scalar_tensor_tensor(out=scr[layer]["top2"][:, :], in0=scr[layer]["rank"][:, :], scalar=2.0, in1=scr[layer]["biased"][:, :],
                                                          op0=ALU.is_lt, op1=ALU.mult))
                chain.step(nc.vector.reduce_sum(scr[layer]["gsc"][:, :], scr[layer]["top2"][:, :].rearrange("p (g i) -> p g i", g=G), axis=AX.X))
                other = scr[layer]["gsc"][:, None, :].to_broadcast([P, G, G])
                mine = scr[layer]["gsc"][:, :, None].to_broadcast([P, G, G])
                chain.post(nc.vector.tensor_tensor(scr[layer]["gbeats"][:, :, 0, :], other, mine, ALU.is_gt))
                chain.step(nc.vector.tensor_tensor(scr[layer]["gbeats"][:, :, 1, :], other, mine, ALU.is_equal))
                chain.step(nc.vector.tensor_tensor(scr[layer]["gbeats"][:, :, 1, :], scr[layer]["gbeats"][:, :, 1, :], earlier[:, :, :], ALU.mult))
                chain.step(nc.vector.reduce_sum(scr[layer]["grank"][:, :], scr[layer]["gbeats"][:, :, :, :].rearrange("p i a j -> p i (a j)"), axis=AX.X))
                chain.step(nc.vector.scalar_tensor_tensor(out=order[:, t, :].rearrange("p (g i) -> p g i", g=G),
                                                          in0=scr[layer]["grank"][:, :, None].to_broadcast([P, G, G]), scalar=4.0,
                                                          in1=scr[layer]["rank"][:, :].rearrange("p (g i) -> p g i", g=G),
                                                          op0=ALU.mult, op1=ALU.add))
                nc.vector.tensor_scalar(sel[:, t, :], order[:, t, :], 2.0, None, ALU.is_lt).then_inc(sel_ready, 1)
                dve.wait_ge(pos_ready, NT * layer + t + 1)
                chain.step(nc.vector.tensor_tensor(posm[:, t, :], sel[:, t, :], ps[:, LGB[layer], 160:160 + E], ALU.mult))
                if t:
                    dve.wait_ge(ids_ready, NT * layer + t)
                slots_hot(dve, layer, posm, t).then_inc(hot_ready, 1)

            def route_ids(layer):
                dve.wait_ge(ids_ready, NT * layer + NT)
                ids = ps[:, IDB[layer], 0:2 * E].rearrange("p (e a) -> p e a", a=2)
                chain.step(nc.vector.tensor_copy(scr[layer]["idsf"][:, :], ids[:, :, 0]))
                nc.vector.tensor_tensor(idx[:, :], scr[layer]["idsf"][:, :], ids[:, :, 1], ALU.add).then_inc(idx_ready, 1)

            def route_gates(layer):
                dve.wait_ge(cnt_ready, layer + 1)
                chain.step(nc.vector.reduce_max(scr[layer]["most_f"][:, :], ps[:, LGB[layer], 192:192 + E], axis=AX.X))
                nc.vector.tensor_copy(most[:, layer:layer + 1], scr[layer]["most_f"][:, :]).then_inc(most_ready, 1)
                for k in range(2):
                    chain.post(nc.vector.tensor_scalar(pick[layer][:, :, k, :], order[:, :, :], float(k), None, ALU.is_equal))
                chain.sync()
                chain.step(nc.vector.tensor_tensor(prod[layer][:, :, :, :], pick[layer][:, :, :, :],
                                                   score[:, :, None, :].to_broadcast([P, NT, 2, E]), ALU.mult))
                chain.step(nc.vector.reduce_sum(gate[:, :, :], prod[layer][:, :, :, :], axis=AX.X))
                chain.step(nc.vector.reduce_sum(scr[layer]["gsum"][:, :], gate[:, :, :], axis=AX.X))
                chain.step(nc.vector.reciprocal(scr[layer]["gsum"][:, :], scr[layer]["gsum"][:, :]))
                chain.step(nc.vector.tensor_tensor(gate[:, :, :], gate[:, :, :],
                                                   scr[layer]["gsum"][:, :, None].to_broadcast([P, NT, 2]), ALU.mult))
                chain.step(nc.vector.tensor_tensor(scr[layer]["place_"][:, :, :], posm[:, :, :],
                                                   row0[:, None, :].to_broadcast([P, NT, E]), ALU.add))
                for k in range(1, NT):
                    chain.step(nc.vector.tensor_scalar(past[layer][:, :, :], posm[:, :, :], float(P * k),
                                                       float((E - 1) * P), ALU.is_gt, ALU.mult))
                    chain.step(nc.vector.tensor_tensor(scr[layer]["place_"][:, :, :], scr[layer]["place_"][:, :, :],
                                                       past[layer][:, :, :], ALU.add))
                chain.step(nc.vector.tensor_tensor(prod[layer][:, :, :, :], pick[layer][:, :, :, :],
                                                   scr[layer]["place_"][:, :, None, :].to_broadcast([P, NT, 2, E]), ALU.mult))
                chain.step(nc.vector.reduce_sum(scr[layer]["rows_f"][:, :, :], prod[layer][:, :, :, :], axis=AX.X))
                nc.vector.tensor_copy(rows[:, :, :], scr[layer]["rows_f"][:, :, :]).then_inc(gates_done, 1)

            def norm_and_route(layer):
                mix_norm(layer, 0)
                for t in range(1, NT):
                    mix_norm(layer, t)
                    route(layer, t - 1)
                route(layer, NT - 1)
                route_ids(layer)

            def experts(layer):
                m0 = E * layer

                def x_lo(c, i=0):
                    dve.wait_ge(xgT_hi_ready, plus(c + m0 + 1, i))
                    nc.vector.tensor_tensor(xgT_lo[:, :, :].rearrange("p k s -> p (k s)"),
                                            ps[:, 5:7, :].rearrange("p b n -> p (b n)"),
                                            xgT_hi[:, :, :].rearrange("p k s -> p (k s)"), ALU.subtract) \
                             .then_inc(xgT_lo_ready, 1)

                def hidden(c, i=0):
                    dve.wait_ge(silu_ready, plus(c + m0 + 1, i))
                    if c + m0:
                        dve.wait_ge(hT_ready, plus(c + m0, i))
                    nc.vector.tensor_tensor(hid[:, :], sgate[:, :], ps[:, 1, :], ALU.mult).then_inc(hid_ready, 1)

                def h_lo(c, i=0):
                    dve.wait_ge(hT_hi_ready, plus(c + m0 + 1, i))
                    nc.vector.tensor_tensor(hT_lo[:, :, :].rearrange("p k s -> p (k s)"), ps[:, 4, :],
                                            hT_hi[:, :, :].rearrange("p k s -> p (k s)"), ALU.subtract) \
                             .then_inc(hT_lo_ready, 1)

                def turn(e, i=0, more_x=True):
                    step = 0 if isinstance(i, int) else 2 * EU
                    n0 = gu0(layer, e + 1) + GU
                    for k in range(GU - 1):
                        own_lo(n0 + k, step, i)
                    hidden(e + 1, i)
                    if more_x:
                        x_lo(e + 2, i)
                    for k in range(GU - 1, EU):
                        if n0 + k < UNITS:
                            own_lo(n0 + k, step, i)
                    h_lo(e + 1, i)

                first = gu0(layer, 0)
                own_lo(first)
                own_lo(first + 2)
                x_lo(0)
                own_lo(first + 4)
                own_lo(first + 6)
                route_gates(layer)
                for k in range(GU - 1):
                    own_lo(gu0(layer, 1) + k)
                hidden(0)
                x_lo(1)
                own_lo(gu0(layer, 1) + GU - 1)
                h_lo(0)
                turn(0)
                turn(1)
                with dve.Fori(0, 6) as i:
                    turn(2, i)
                    turn(3, i)
                turn(14, more_x=False)
                if layer == 0:
                    for k in range(4):
                        own_lo(U0 + 4 + k)

            def combine(layer):
                def x_lo(t):
                    for h in range(2):
                        dve.wait_ge(xt_hi, 4 + 2 * t + h + 1)
                        dst = slice(4 * h, 4 * h + 4), slice(t * P, (t + 1) * P)
                        nc.vector.tensor_tensor(xT_lo[:, dst[0], dst[1]],
                                                ps[:, TRB[0] + h, :].rearrange("p (k s) -> p k s", k=4),
                                                xT_hi[:, dst[0], dst[1]], ALU.subtract).then_inc(xt_lo, 1)

                for t in range(NT):
                    dve.wait_ge(yg_scaled, NT * layer + t + 1)
                    chain.step(nc.vector.scalar_tensor_tensor(out=X[:, t, :], in0=X[:, t, :], scalar=ALPHA,
                                                              in1=yg[:, t, 0, :], op0=ALU.mult, op1=ALU.add))
                    chain.step(nc.vector.scalar_tensor_tensor(out=X[:, t, :], in0=yg[:, t, 1, :],
                                                              scalar=gate[:, t, 1:2], in1=X[:, t, :],
                                                              op0=ALU.mult, op1=ALU.add))
                    norm(8 * layer + 4 + t, t, ffn_par, 2 + 2 * layer)
                    if layer == 0 and t:
                        x_lo(t - 1)
                if layer == 0:
                    x_lo(NT - 1)

            norm_and_route(0)
            experts(0)
            overflow_dve(dve, 0)
            combine(0)

            with dve.Fori(0, 2) as i:
                for a in range(8):
                    own_lo(U0 + 8 + a, RING, i)
            for nb in range(4):
                for t in range(NT):
                    dve.wait_ge(v_copied, NT * nb + t + 1)
                    chain.post(nc.vector.bn_stats(v_parts[:, t, nb, :], V[:, 4 * nb:4 * nb + 4, t, :]))
                for k in range(4):
                    if nb < 3:
                        own_lo(V0 + 8 + 4 * nb + k)
            chain.sync()
            for t in range(NT):
                ins = nc.vector.bn_aggr(mv[:, t, :], v_parts[:, t, :, :].rearrange("p a b -> p (a b)"))
                if t < NT - 1:
                    chain.post(ins)
            ins.then_inc(v_stats, 1)
            dve.wait_ge(v_root, 1)
            chain.step(nc.vector.reciprocal(rstd[:, :], std[:, :]))
            nc.vector.scalar_tensor_tensor(out=nmr[:, :], in0=mv[:, :, 0], scalar=-1.0, in1=rstd[:, :],
                                           op0=ALU.mult, op1=ALU.mult).then_inc(v_stats, 1)
            for t in (0, 1):
                nc.vector.tensor_scalar(V[:, :, t, :], V[:, :, t, :], mv[:, t, 0:1], rstd[:, t:t + 1],
                                        ALU.subtract, ALU.mult).then_inc(v_normed, 1)
            for k in range(4):
                own_lo(V0 + 20 + k)
            dve.wait_ge(bs_in, 16)
            dve.wait_ge(ws_copied, 2)

            def g_lo(j):
                dve.wait_ge(g_hi_ready, j + 1)
                nc.vector.tensor_tensor(gated(j)[1], U[:, j, :], gated(j)[0], ALU.subtract).then_inc(g_lo_ready, 1)

            for j in range(NC):
                h = j // 2
                chain.step(nc.vector.scalar_tensor_tensor(out=rank1[:, :], in0=ws_sum[:, h, :], scalar=vb[:, j:j + 1],
                                                          in1=bsb[:, h, :], op0=ALU.mult, op1=ALU.add))
                dve.wait_ge(sg_ready, j + 1)
                nc.vector.scalar_tensor_tensor(out=V[:, j, :, :], in0=ps[:, 4 + j % 2, :].rearrange("p (t i) -> p t i", t=NT),
                                               scalar=vg[:, j:j + 1],
                                               in1=rank1[:, None, :].to_broadcast([P, NT, P]),
                                               op0=ALU.mult, op1=ALU.add).then_inc(sg_taken, 1)
                dve.wait_ge(sg_taken, j + 1)
                nc.vector.tensor_tensor(U[:, j, :], U[:, j, :], V[:, j, :, :].rearrange("p t i -> p (t i)"), ALU.mult) \
                         .then_inc(g_ready, 1)
                if j:
                    g_lo(j - 1)
                if j >= 4 and j % 2 == 0:
                    own_lo(SO0 + 8 + (j - 4) // 2)
            g_lo(NC - 1)
            own_lo(SO0 + 14)
            own_lo(SO0 + 15)
            dve.wait_ge(x_back, 16)
            dve.wait_ge(unit_used, SO0 + 8)
            for t in range(NT):
                nc.vector.scalar_tensor_tensor(out=X[:, t, 0:BANK], in0=X[:, t, 0:BANK], scalar=ALPHA, in1=ps[:, t, :],
                                               op0=ALU.mult, op1=ALU.add).then_inc(nh0_taken, 1)
            dve.wait_ge(nh0_taken, NT)

            norm_and_route(1)
            experts(1)
            overflow_dve(dve, 1)
            combine(1)

        @block.tensor
        def _(pe):
            pe.wait_ge(consts, 1)
            pe.wait_ge(ws_masked, 1)
            for h in range(H):
                ins = nc.tensor.transpose(ps[:, h // 4, (h % 4) * P:(h % 4 + 1) * P], bsb[:, h, :], ident[:, :])
            ins.then_inc(ws_tr, 1)
            pe.wait_ge(ws_copied, 1)
            for b in range(2):
                ins = nc.tensor.matmul(ps[:, 2 + b, :], ones_f[:, :], wcT[:, 4 * b:4 * b + 4, :].rearrange("p h i -> p (h i)"),
                                       start=True, stop=True)
            ins.then_inc(ws_summed, 1)
            pe.wait_ge(ws_copied, 2)

            def conv_tile(c, i=0):
                j = plus(c, i)
                if c >= 2:
                    pe.wait_ge(bz_ready, j - 1)
                for g in range(3):
                    n = 3 * c + g
                    s = slot_of(n)
                    wait_lo(pe, n, CRING, i)
                    for k in range(KD):
                        if c == 0 and g == 0 and k % 2 == 0:
                            pe.wait_ge(xt_lo, k // 2 + 1)
                        w = slice(k * P, (k + 1) * P)
                        ins = passes(ps[:, 3 * (c % 2) + g, :], hi[:, s, w], lo[:, s, w], xT_hi[:, k, :], xT_lo[:, k, :],
                                     k == 0, k == KD - 1)
                    ins.then_inc(unit_used, 1)

            conv_tile(0)
            conv_tile(1)
            with pe.Fori(0, 3) as i:
                conv_tile(2, i)
                conv_tile(3, i)

            def mix(layer, t, between):
                if layer == 0:
                    steps = [(k, h, OUT0 + k) for k in range(KD) for h in range(2)]
                else:
                    steps = [(k, 0, SO0 + 8 + k // 2) for k in range(NC)]
                tok = slice(t * P, (t + 1) * P)
                for m, (k, h, n) in enumerate(steps):
                    s = slot_of(n)
                    if layer == 0:
                        if t == 0 and h == 0:
                            pe.wait_ge(bz_lo_ready, k + 1)
                            wait_lo(pe, n)
                        if t == 1 and m == 0:
                            pe.wait_ge(bz_ready, KD)
                        if t > 1 and m == 0:
                            pe.wait_ge(mix_taken, t - 1)
                        a_hi, a_lo = bz_hi[:, k, tok], bz_lo[:, k, tok]
                        cols, bank = slice(h * BANK, (h + 1) * BANK), (6, 0)[t % 2] + h
                        last_of_unit = h == 1
                        first, last = k == 0, k == KD - 1
                    else:
                        if t == 0 and k % 2 == 0:
                            wait_lo(pe, n)
                        a_hi, a_lo = (part[:, tok] for part in gated(k))
                        cols, bank = slice((k % 2) * BANK, (k % 2 + 1) * BANK), 4 + t
                        last_of_unit = k % 2 == 1
                        first, last = k == 0, k == NC - 1
                    ins = passes(ps[:, bank, :], a_hi, a_lo, hi[:, s, cols], lo[:, s, cols], first, last)
                    if t == NT - 1 and last_of_unit:
                        ins.then_inc(unit_used, 1)
                    elif t < NT - 1 and m == len(steps) - 1:
                        ins.then_inc(mix_ready, 1)
                    if m % 4 == 3:
                        for f in between.get(m // 4, ()):
                            f()

            def turn_tile(q, t, bank):
                pe.wait_ge(normed, q + 1)
                for h in range(2):
                    for k in range(4):
                        ins = nc.tensor.transpose(ps[:, bank + h, k * P:(k + 1) * P],
                                                  X[:, t, (4 * h + k) * P:(4 * h + k + 1) * P], ident[:, :])
                    ins.then_inc(tr_ready, 1)

            def logits(layer, t):
                pe.wait_ge(tr_taken, 8 * layer + 2 * t + 2)
                if t:
                    pe.wait_ge(s_ready, NT * layer + t)
                for k in range(KD):
                    ins = nc.tensor.matmul(ps[0:E, logit_bank(layer, t), 0:P], rw[:, k, :], xTt[layer][:, k, :],
                                           start=(k == 0), stop=(k == KD - 1))
                ins.then_inc(logit_ready, 1)

            def by_token(layer, t):
                pe.wait_ge(sig_ready, NT * layer + t + 1)
                nc.tensor.transpose(ps[:, LGB[layer], P:P + E], scr[layer]["sig"][:, :], ident[0:E, 0:E]).then_inc(s_ready, 1)

            def positions(layer, t):
                pe.wait_ge(sel_ready, NT * layer + t + 1)
                dst = ps[:, LGB[layer], 160:160 + E]
                for u in range(t):
                    nc.tensor.matmul(dst, ones_b[:, :], sel[:, u, :], start=(u == 0), stop=False)
                nc.tensor.matmul(dst, tri[:, :], sel[:, t, :], start=(t == 0), stop=True).then_inc(pos_ready, 1)

            def ids(layer, t):
                pe.wait_ge(hot_ready, NT * layer + t + 1)
                ids_of(hot[layer], IDB[layer], t).then_inc(ids_ready, 1)

            def ids_of(onehot, bank, t):
                for e in range(E):
                    ins = nc.tensor.matmul(ps[:, bank, 2 * e:2 * e + 2], onehot[:, e, :], tok_id[:, t, :],
                                           start=(t == 0 and e == 0), stop=(t == NT - 1), skip_group_check=True)
                return ins

            def mix_and_route(layer):
                T = lambda t: lambda: turn_tile(8 * layer + t, t, TRB[layer])
                L = lambda t: lambda: logits(layer, t)
                B = lambda t: lambda: by_token(layer, t)
                C = lambda t: lambda: positions(layer, t)
                I = lambda t: lambda: ids(layer, t)
                mix(layer, 0, {})
                mix(layer, 1, {3: (T(0),)})
                mix(layer, 2, {0: (L(0),), 1: (B(0),), 2: (C(0),), 3: (I(0), T(1))})
                mix(layer, 3, {0: (L(1),), 1: (B(1),), 2: (C(1),), 3: (I(1), T(2))})
                for f in (L(2), B(2), T(3), L(3), C(2), I(2), B(3), C(3), I(3)):
                    f()
                for u in range(NT):
                    ins = nc.tensor.matmul(ps[:, LGB[layer], 192:192 + E], ones_b[:, :], sel[:, u, :],
                                           start=(u == 0), stop=(u == NT - 1))
                ins.then_inc(cnt_ready, 1)

            def experts(layer):
                m0 = E * layer

                def turn_x(c, i=0):
                    pe.wait_ge(xg_in[c % 2], plus(16 * ((c + m0) // 2 + 1), i, 16))
                    if c + m0:
                        pe.wait_ge(xgT_lo_ready, plus(c + m0, i))
                    for k in range(KD):
                        ins = nc.tensor.transpose(ps[:, 5 + k // 4, (k % 4) * P:(k % 4 + 1) * P],
                                                  xg[:, c % 2, k * P:(k + 1) * P], ident[:, :])
                    ins.then_inc(xgT_ready, 1)

                def gate_up(c, step=0, i=0):
                    pe.wait_ge(xgT_lo_ready, plus(c + m0 + 1, i))
                    if c + m0:
                        pe.wait_ge(hid_ready, plus(c + m0, i))
                    for k in range(GU):
                        n = gu0(layer, c) + k
                        s = slot_of(n)
                        wait_lo(pe, n, step, i)
                        for h in range(2):
                            cols = slice(h * F, (h + 1) * F)
                            ins = passes(ps[:, h, :], xgT_hi[:, k, :], xgT_lo[:, k, :], hi[:, s, cols], lo[:, s, cols],
                                         k == 0, k == GU - 1)
                        ins.then_inc(unit_used, 1)

                def turn_h(c, i=0):
                    pe.wait_ge(hid_ready, plus(c + m0 + 1, i))
                    if c + m0:
                        pe.wait_ge(hT_lo_ready, plus(c + m0, i))
                    for k in range(KF):
                        ins = nc.tensor.transpose(ps[:, 4, k * P:(k + 1) * P], hid[:, k * P:(k + 1) * P], ident[:, :])
                    ins.then_inc(hT_ready, 1)

                def down(c, step=0, i=0):
                    pe.wait_ge(hT_lo_ready, plus(c + m0 + 1, i))
                    if c + m0:
                        pe.wait_ge(y_copied, plus(c + m0, i))
                    for k in range(DN):
                        n = dn0(layer, c) + k
                        s = slot_of(n)
                        wait_lo(pe, n, step, i)
                        for h in range(2):
                            cols = slice(h * BANK, (h + 1) * BANK)
                            ins = passes(ps[:, 2 + h, :], hT_hi[:, k, :], hT_lo[:, k, :], hi[:, s, cols], lo[:, s, cols],
                                         k == 0, k == DN - 1)
                        ins.then_inc(unit_used, 1)

                def turn(e, i=0, more_x=True):
                    step = 0 if isinstance(i, int) else 2 * EU
                    gate_up(e + 1, step, i)
                    if more_x:
                        turn_x(e + 2, i)
                    down(e, step, i)
                    turn_h(e + 1, i)

                turn_x(0)
                gate_up(0)
                turn_x(1)
                turn_h(0)
                turn(0)
                turn(1)
                with pe.Fori(0, 6) as i:
                    turn(2, i)
                    turn(3, i)
                turn(14, more_x=False)
                down(15)

            mix_and_route(0)
            experts(0)
            overflow_pe(pe, 0, ids_of)
            for t in range(NT):
                if t:
                    pe.wait_ge(xt_lo, 4 + 2 * t)
                turn_tile(4 + t, t, TRB[0])

            pe.wait_ge(xt_lo, 4 + 2 * NT)
            with pe.Fori(0, 2) as i:
                for a in range(8):
                    n, s = U0 + a, slot_of(U0 + a)
                    if a >= 2:
                        pe.wait_ge(u_copied, plus(a, i, 8))
                    else:
                        pe.wait_ge(u_copied, i * (7 + a) + 1)
                    wait_lo(pe, n, RING, i)
                    for k in range(KD):
                        w = slice(k * P, (k + 1) * P)
                        ins = passes(ps[:, a % 2, :], hi[:, s, w], lo[:, s, w], xT_hi[:, k, :], xT_lo[:, k, :],
                                     k == 0, k == KD - 1)
                    ins.then_inc(unit_used, 1)
            pe.wait_ge(u_copied, NC + 1)
            for nb in range(4):
                for m in range(4):
                    n, s = V0 + 4 * nb + m, slot_of(V0 + 4 * nb + m)
                    wait_lo(pe, n)
                    for kk in range(2):
                        k = 2 * m + kk
                        for t in range(NT):
                            if nb >= 2 and k == 0:
                                pe.wait_ge(v_copied, NT * (nb - 2) + t + 1)
                            tok, cols = slice(t * P, (t + 1) * P), slice(kk * BANK, (kk + 1) * BANK)
                            ins = passes(ps[:, (nb % 2) * 4 + t, :], xT_hi[:, k, tok], xT_lo[:, k, tok],
                                         hi[:, s, cols], lo[:, s, cols], k == 0, k == KD - 1)
                            if k == KD - 1 and t < NT - 1:
                                ins.then_inc(v_ready, 1)
                    ins.then_inc(unit_used, 1)

            def spatial(j):
                if j >= 2:
                    pe.wait_ge(sg_taken, j - 1)
                for t in range(NT):
                    ins = nc.tensor.matmul(ps[:, 4 + j % 2, t * P:(t + 1) * P], V[:, j, t, :], wcT[:, j // 2, :],
                                           start=True, stop=True)
                ins.then_inc(sg_ready, 1)

            pe.wait_ge(v_normed, 2)
            pe.wait_ge(v_normed_a, 2)
            for j in range(4):
                spatial(j)
            for m in range(8):
                n, s = SO0 + m, slot_of(SO0 + m)
                pe.wait_ge(g_lo_ready, 2 * m + 2)
                wait_lo(pe, n)
                for kk in range(2):
                    k = 2 * m + kk
                    for t in range(NT):
                        tok, cols = slice(t * P, (t + 1) * P), slice(kk * BANK, (kk + 1) * BANK)
                        a_hi, a_lo = (part[:, tok] for part in gated(k))
                        ins = passes(ps[:, t, :], a_hi, a_lo, hi[:, s, cols], lo[:, s, cols], k == 0, k == NC - 1)
                ins.then_inc(unit_used, 1)
                for j in (2 * m + 4, 2 * m + 5):
                    if j < NC:
                        spatial(j)
            pe.wait_ge(sg_taken, NC)
            mix_and_route(1)
            experts(1)
            overflow_pe(pe, 1, ids_of)


def _pairs(units):
    n = units.shape[0] // 2
    return units.reshape(n, 2, P, UN).transpose(0, 2, 1, 3).reshape(n, P, 2 * UN)


def kernel(**inputs):
    import numpy as np
    from concourse import bacc
    from concourse.bass_utils import run_bass_kernel_spmd

    a = {k: np.asarray(v) for k, v in inputs.items()}
    x = a["x"][0]
    cols = lambda w: w.reshape(KD, P, -1, P).transpose(2, 1, 0, 3).reshape(-1, P, UN)
    conv_in = cols(a["a_w_in"][0]).reshape(3, KD, P, UN).transpose(1, 0, 2, 3).reshape(N_CONV, P, UN)
    w_dense0 = _pairs(np.concatenate([conv_in, a["a_w_out"][0].reshape(KD, P, UN)]))
    b_in = a["b_w_in"][0]
    blocks = lambda w: (w.reshape(w.shape[0] // (2 * P), 2, P, w.shape[1] // BANK, BANK)
                        .transpose(3, 0, 2, 1, 4).reshape(-1, P, UN))
    w_dense1 = _pairs(np.concatenate([cols(b_in[:, :SGU]), blocks(b_in[:, SGU:]), blocks(a["b_w_out"][0])]))
    gate_up = np.stack([a["moe_w_gate"], a["moe_w_up"]], axis=3)
    gate_up = gate_up.reshape(2, E, GU // 2, 2, P, UN)
    down = a["moe_w_down"].reshape(2, E, DN // 2, 2, P, UN)
    w_moe = np.concatenate([gate_up, down], axis=2).transpose(0, 1, 2, 4, 3, 5).reshape(2, E, EU // 2, P, 2 * UN)
    data = {
        "x": x,
        "x_t": x.T.reshape(4, 2, P, S).transpose(0, 2, 1, 3).reshape(4, P, 2 * S),
        "w_dense0": w_dense0,
        "w_moe": w_moe,
        "w_dense1": w_dense1,
        "conv_w": a["a_conv_w"][0].reshape(3, KD, P).transpose(2, 1, 0),
        "router_w": a["router_w"].reshape(KD, P, E).transpose(1, 0, 2),
        "router_bias": a["router_bias"],
        "w_s": a["b_ws"][0].transpose(1, 0, 2),
        "b_s": a["b_bs"][0].reshape(H * P),
        "v_gain": a["b_ln_g"][0].reshape(NC, P).T,
        "v_bias": a["b_ln_b"][0].reshape(NC, P).T,
        "ln_par": np.stack([np.stack([a["ln_mix_g"], a["ln_mix_b"]], 1), np.stack([a["ln_ffn_g"], a["ln_ffn_b"]], 1)], 1),
    }
    nc = bacc.Bacc("TRN2", target_bir_lowering=False, num_devices=1)
    arrays, args = {}, []
    for name, v in data.items():
        v = np.ascontiguousarray(v)
        arrays["in_" + name] = v
        args.append(nc.dram_tensor("in_" + name, v.shape, mybir.dt.from_np(v.dtype), kind="ExternalInput").ap())
    out = nc.dram_tensor("out", [S, D], F32, kind="ExternalOutput").ap()
    hybrid_decoder(nc, *args, out)
    r = run_bass_kernel_spmd(nc, [arrays], core_ids=[0])
    return r.results[0]["out"].reshape(1, S, D)
```

```python
import concourse.bass as bass
from concourse import mybir
from contextlib import ExitStack

F32 = mybir.dt.float32
F32R = mybir.dt.float32r
BF16 = mybir.dt.bfloat16
I32 = mybir.dt.int32
ALU = mybir.AluOpType
ACT = mybir.ActivationFunctionType
AX = mybir.AxisListType

P = 128
D = 1024
S = 512
NT = S // P
KD = D // P
BANK = 512
E = 16
T = 112
TILES = -(-S // T)
G = 4
F = 512
KF = F // P
SGU = 2048
NC = SGU // P
H = 8
ALPHA = 4.0 ** 0.25
EPS = 1e-5
KB = 1024

UN = 1024
RING = 8
N_CONV = 3 * KD
CRING = 6
OUT0 = N_CONV
GU, DN = KD, KF
EU = GU + DN
MOE = [OUT0 + KD, 0]
U0 = MOE[0] + E * EU
V0 = U0 + NC
SO0 = V0 + 16
MOE[1] = SO0 + 16
UNITS = MOE[1] + E * EU


def gu0(layer, e):
    return MOE[layer] + (0 if e == 0 else GU + EU * (e - 1))


def dn0(layer, e):
    return MOE[layer] + (GU + EU * e + GU if e < E - 1 else GU + EU * e)


def slot_of(n):
    return n % CRING if n < N_CONV else (n + CRING - N_CONV % RING) % RING


MORE = 4
RAW_ORDER = [slot_of(MOE[0] + k) for k in range(RING)] + [RING + k for k in range(MORE)]


def layer_of(n):
    return next((l for l in (0, 1) if MOE[l] <= n < MOE[l] + E * EU), None)


def raw_slot(n):
    return slot_of(n) if layer_of(n) is None else RAW_ORDER[(n - MOE[layer_of(n)]) % len(RAW_ORDER)]


def last_users(slot):
    last, out = {}, []
    for n in range(UNITS):
        out.append(last.get(slot(n)))
        last[slot(n)] = n
    return out


BEFORE, RAW_BEFORE = last_users(slot_of), last_users(raw_slot)


def pool_owned():
    own = [False] * UNITS
    for layer in (0, 1):
        for k in range(GU - 1):
            own[gu0(layer, 0) + k] = True
        for e in range(1, E):
            own[gu0(layer, e) + 3] = True
        for e in range(E):
            own[dn0(layer, e) + 3] = True
    return own


POOL = pool_owned()
LO_DVE = [sum(not x for x in POOL[:n + 1]) for n in range(UNITS)]
LO_POOL = [sum(POOL[:n + 1]) for n in range(UNITS)]
INDEX = list(range(UNITS))


def pair_count():
    seen, out = [0] * ((RING + MORE) // 2), []
    for n in range(0, UNITS, 2):
        seen[raw_slot(n) // 2] += 1
        out += [seen[raw_slot(n) // 2]] * 2
    return out


PAIRS = pair_count()


def at(count, n, step, i):
    if isinstance(i, int):
        return count[n + step * i]
    return i * (count[n + step] - count[n]) + count[n]


class Chain:

    def __init__(self, eng, sem):
        self.eng, self.sem, self.n, self.i, self.per = eng, sem, 0, 0, 0

    def post(self, ins):
        ins.then_inc(self.sem, 1)
        self.n += 1

    def sync(self):
        self.eng.wait_ge(self.sem, self.n if isinstance(self.i, int) else self.i * self.per + self.n)

    def step(self, ins):
        self.post(ins)
        self.sync()

    def enter(self, i, per):
        self.i, self.per, self.start = i, per, self.n

    def leave(self, turns):
        assert self.n - self.start == self.per, (self.n - self.start, self.per)
        self.i, self.n = 0, self.start + self.per * turns


def plus(c, i, k=2):
    return k * i + c if isinstance(i, int) else i * k + c


def is_zero(n):
    return isinstance(n, int) and n == 0


def hybrid_decoder(nc, x, x_t, w_dense0, w_moe, w_dense1, conv_w, router_w, router_bias,
                   w_s, b_s, v_gain, v_bias, ln_par, out):
    ctx = ExitStack()
    with ctx:
        base = -(-nc.sbuf_base // 64) * 64
        top = [base]

        def place(name, shape, dt, offset=None):
            size = 2 if dt == BF16 else 4
            for d in shape[1:]:
                size *= d
            if offset is None:
                offset = top[0]
                top[0] += -(-size // 32) * 32
                assert top[0] <= nc.sbuf_usable_end, (name, top[0], nc.sbuf_usable_end)
            else:
                offset += zone
            return nc.alloc_sbuf_tensor_at(name, shape, dt, offset=offset)

        raw = place("raw", [P, RING, UN], F32)
        hi = place("hi", [P, RING, UN], F32R)
        lo = place("lo", [P, RING, UN], F32R)
        zone = top[0]
        top[0] += 96 * KB

        X = place("X", [P, NT, D], F32, 80 * KB)
        xT_hi = place("xT_hi", [P, KD, S], F32R, 0)
        xT_lo = place("xT_lo", [P, KD, S], F32R, 16 * KB)
        xT_raw = place("xT_raw", [P, KD, S], F32, 32 * KB)
        bz_hi = place("bz_hi", [P, KD, S], F32R, 32 * KB)
        bz_lo = place("bz_lo", [P, KD, S], F32R, 48 * KB)
        cgate = place("cgate", [P, S], F32, 64 * KB)
        ch = place("ch", [P, 2 + S], F32, 66 * KB)
        z = place("z", [P, S], F32, 69 * KB)
        U = place("U", [P, NC, S], F32, 32 * KB)
        V = place("V", [P, NC, NT, P], F32, 64 * KB)
        g2_hi = place("g2_hi", [P, NC // 2, S], F32R, 32 * KB)
        g2_lo = place("g2_lo", [P, NC // 2, S], F32R, 64 * KB)
        xTt = [place(f"xTt{l}", [P, KD, P], F32, o) for l, o in ((0, 8 * KB), (1, 56 * KB))]
        mix_par = [place(f"mix_par{l}", [P, 2, D], F32, o) for l, o in ((0, 72 * KB), (1, 48 * KB))]
        ffn_par = [place(f"ffn_par{l}", [P, 2, D], F32, o) for l, o in ((0, 72 * KB), (1, 56 * KB))]
        raw_more = [place(f"raw_more{l}", [P, MORE, UN], F32, o) for l, o in ((0, 40 * KB), (1, 64 * KB))]
        xg = place("xg", [P, 2, D], F32, 8 * KB)
        xgT_hi = place("xgT_hi", [P, KD, P], F32R, 16 * KB)
        xgT_lo = place("xgT_lo", [P, KD, P], F32R, 20 * KB)
        sgate = place("sgate", [P, F], F32, 24 * KB)
        hid = place("hid", [P, F], F32, 26 * KB)
        hT_hi = place("hT_hi", [P, KF, P], F32R, 28 * KB)
        hT_lo = place("hT_lo", [P, KF, P], F32R, 30 * KB)
        y = place("y", [P, 2, D], F32, 32 * KB)
        w_over = place("w_over", [P, 2, 2 * UN], F32, 40 * KB)
        y_over = place("y_over", [P, D], F32, 4 * KB)
        x_over = place("x_over", [P, KD, P], F32, 64 * KB)
        h_over = place("h_over", [P, KF, P], F32, 68 * KB)

        ident = place("ident", [P, P], F32)
        ones_f = place("ones_f", [P, P], F32, 68 * KB + 256)
        ones_b = place("ones_b", [P, P], BF16)
        tri = place("tri", [P, P], BF16)
        iota_s = place("iota_s", [P, P], BF16)
        tok_par = place("tok_par", [P, NT, E, 6], BF16)
        earlier = place("earlier", [P, G, G], F32)
        no_row = place("no_row", [P, 2], F32)
        eps = place("eps", [P, 1], F32)
        warm = place("warm", [P, 1], F32)
        rw = place("rw", [P, KD, E], F32)
        rbias = place("rbias", [P, E], F32)
        cw = place("cw", [P, KD, 3], F32)
        wcT_at = top[0]
        wcT = place("wcT", [P, H, P], F32)
        ws_sum_at = top[0]
        ws_sum = place("ws_sum", [P, H, P], F32)
        bsb_at = top[0] - zone
        bsb = place("bsb", [P, H, P], F32)
        vg = place("vg", [P, NC], F32)
        vb = place("vb", [P, NC], F32)
        stats = place("stats", [P, 2, 6], F32)
        hot = [[place(f"hot{l}_{t}", [P, E, T], BF16, o) for t, o in enumerate(offs)]
               for l, offs in ((0, (0, 4 * KB, 32 * KB, 36 * KB)),
                               (1, (60 * KB, ws_sum_at - zone, 32 * KB, 36 * KB)))]
        mv = place("mv", [P, NT, 2], F32)
        std = place("std", [P, NT], F32)
        rstd = place("rstd", [P, NT], F32)
        nmr = place("nmr", [P, NT], F32)
        score_at = top[0]
        score = place("score", [P, NT, E], F32)
        order = place("order", [P, NT, E], F32)
        rank1 = nc.alloc_sbuf_tensor_at("rank1", [P, P], F32, offset=score_at)
        v_parts = nc.alloc_sbuf_tensor_at("v_parts", [P, NT, 4, 6], F32, offset=score_at)
        most = place("most", [P, 2], I32)
        sel = place("sel", [P, NT, E], BF16, bsb_at)
        posm = place("posm", [P, NT, E], F32, bsb_at + 128)
        idx = place("idx", [P, E], I32, bsb_at + 384)
        idx_col = place("idx_col", [P, 2], I32, bsb_at + 448)
        out_col = place("out_col", [P, 1], I32, bsb_at + 480)
        slot_gate = place("slot_gate", [P, E], F32, bsb_at + 512)

        iota_i = place("iota_i", [P, P], I32, 71 * KB + 256)
        def scratch(layer):
            at_ = 70 * KB if layer == 0 else wcT_at - zone
            out = {}
            for name, shape, dt in (
                    ("sig", [E, P], F32),
                    ("biased", [P, E], F32),
                    ("beats", [P, G, G, 2, G], F32),
                    ("rank", [P, E], F32),
                    ("top2", [P, E], F32),
                    ("gsc", [P, G], F32),
                    ("gbeats", [P, G, 2, G], F32),
                    ("grank", [P, G], F32),
                    ("most_f", [P, 1], F32),
                    ("by_slot", [P, E, 6], F32),
                    ("gsum", [P, NT], F32),
                    ("gates", [P, NT, E], F32),
                    ("place_", [P, NT, E], F32)):
                size = 4
                for d in shape[1:]:
                    size *= d
                if name == "by_slot" and layer == 0:
                    at_ = 60 * KB
                tensor = nc.alloc_sbuf_tensor_at(f"{name}{layer}", shape, dt, offset=zone + at_)
                at_ += -(-size // 32) * 32
                out[name] = tensor
            return out

        scr = [scratch(0), scratch(1)]

        ps = ctx.enter_context(nc.psum_tensor("ps", [P, 8, BANK], F32))
        x_rows = nc.dram_tensor("x_rows", [S, D], F32)
        x_mid = nc.dram_tensor("x_mid", [S, D], F32)
        acc = [nc.dram_tensor(f"acc{l}", [S + P, D], F32) for l in (0, 1)]

        def sem(name):
            return ctx.enter_context(nc.semaphore(name))

        raw_in = [sem(f"raw_in{s}") for s in range((RING + MORE) // 2)]
        hi_ready = sem("hi_ready")
        lo_ready = sem("lo_ready")
        lo_ready_p = sem("lo_ready_p")
        unit_used = sem("unit_used")
        xt_in = [sem(f"xt_in{c}") for c in range(4)]
        x_in = sem("x_in")
        small_in = sem("small_in")
        ws_in = sem("ws_in")
        par_in = sem("par_in")
        consts = sem("consts")
        dve_step = sem("dve_step")
        pool_step = sem("pool_step")
        act_step = sem("act_step")
        xt_hi = sem("xt_hi")
        xt_lo = sem("xt_lo")
        ws_masked = sem("ws_masked")
        ws_tr = sem("ws_tr")
        ws_copied = sem("ws_copied")
        ws_summed = sem("ws_summed")
        c_ready = sem("c_ready")
        bz_ready = sem("bz_ready")
        bz_hi_ready = sem("bz_hi_ready")
        bz_lo_ready = sem("bz_lo_ready")
        mix_ready = sem("mix_ready")
        mix_taken = sem("mix_taken")
        var_ready = sem("var_ready")
        std_ready = sem("std_ready")
        normed = sem("normed")
        tr_ready = sem("tr_ready")
        tr_taken = sem("tr_taken")
        logit_ready = sem("logit_ready")
        sig_ready = sem("sig_ready")
        s_ready = sem("s_ready")
        sel_ready = sem("sel_ready")
        pos_ready = sem("pos_ready")
        hot_ready = sem("hot_ready")
        ids_ready = sem("ids_ready")
        idx_ready = sem("idx_ready")
        xrow_out = [sem(f"xrow_out{t}") for t in range(NT)]
        xmid_out = sem("xmid_out")
        out_done = sem("out_done")
        xg_in = [sem(f"xg_in{b}") for b in range(2)]
        xgT_ready = sem("xgT_ready")
        xgT_hi_ready = sem("xgT_hi_ready")
        xgT_lo_ready = sem("xgT_lo_ready")
        silu_ready = sem("silu_ready")
        hid_ready = sem("hid_ready")
        hT_ready = sem("hT_ready")
        hT_hi_ready = sem("hT_hi_ready")
        hT_lo_ready = sem("hT_lo_ready")
        y_copied = sem("y_copied")
        acc_out = sem("acc_out")
        y_out = sem("y_out")
        gates_done = sem("gates_done")
        gates_by_slot = sem("gates_by_slot")
        slot_gate_ready = sem("slot_gate_ready")
        summed = sem("summed")
        acc_in = [sem(f"acc_in{t}") for t in range(NT)]
        u_copied = sem("u_copied")
        v_ready = sem("v_ready")
        v_copied = sem("v_copied")
        v_stats = sem("v_stats")
        v_root = sem("v_root")
        g_ready = sem("g_ready")
        bs_in = sem("bs_in")
        cnt_ready = sem("cnt_ready")
        most_ready = sem("most_ready")
        v_normed = sem("v_normed")
        v_normed_a = sem("v_normed_a")
        sg_ready = sem("sg_ready")
        sg_taken = sem("sg_taken")
        g_hi_ready = sem("g_hi_ready")
        g_lo_ready = sem("g_lo_ready")
        nh0_taken = sem("nh0_taken")
        x_back = sem("x_back")

        block = ctx.enter_context(nc.Block())

        def lo_sem(n):
            return lo_ready_p if POOL[n] else lo_ready

        def wait_lo(eng, n, step=0, i=0):
            eng.wait_ge(lo_sem(n), at(LO_POOL if POOL[n] else LO_DVE, n, step, i))

        def lo_count(eng, n, step, i, reg):
            value = at(LO_POOL if POOL[n] else LO_DVE, n, step, i)
            if isinstance(value, int):
                return value
            eng.reg_mov(reg, value)
            return reg

        def raw_units(n, count=1):
            s = raw_slot(n)
            if s < RING:
                return raw[:, s:s + count, :]
            return raw_more[layer_of(n)][:, s - RING:s - RING + count, :]

        def flat(slots_):
            return slots_.rearrange("p u n -> p (u n)")

        def split_hi(act, n, step=0, i=0):
            s = slot_of(n)
            if n % 2 == 0:
                act.wait_ge(raw_in[raw_slot(n) // 2], at(PAIRS, n, step, i) * 16)
            if BEFORE[n] is not None:
                act.wait_ge(unit_used, at(INDEX, BEFORE[n], step, i) + 1)
            nc.scalar.activation(hi[:, s, :], flat(raw_units(n)), ACT.Copy).then_inc(hi_ready, 1)

        def split_lo(eng, n, step=0, i=0, count=None):
            s = slot_of(n)
            eng.wait_ge(hi_ready, at(INDEX, n, step, i) + 1 if count is None else count)
            eng.tensor_tensor(lo[:, s, :], flat(raw_units(n)), hi[:, s, :], ALU.subtract) \
               .then_inc(lo_ready_p if POOL[n] else lo_ready, 1)

        def passes(out_, a_hi, a_lo, b_hi, b_lo, first, last):
            nc.tensor.matmul(out_, a_hi, b_hi, start=first, stop=False)
            nc.tensor.matmul(out_, a_hi, b_lo, start=False, stop=False)
            return nc.tensor.matmul(out_, a_lo, b_hi, start=False, stop=last)

        TRB = (2, 0)
        TRF = (2, 4, 2, 2)
        LGB = (4, 2)
        IDB = (5, 3)

        V_PARTS = (slice(0, 4), slice(4, NC))
        UB = (0, 1, 4, 5, 6, 7, 2, 3)

        TR_MIX, TR_FFN = (0, 4 * NT), 2 * NT


        def tile_of(t, j):
            return t[:, j, :] if isinstance(j, int) else t[:, bass.ds(j, 1), :].rearrange("p a s -> p (a s)")

        def gated(j):
            if j < NC // 2:
                return xT_hi[:, j, :], xT_lo[:, j, :]
            return g2_hi[:, j - NC // 2, :], g2_lo[:, j - NC // 2, :]

        def slots_hot(eng, out_, pos, t):
            return eng.tensor_tensor(out_[:, :, :], iota_s[:, None, 0:T].to_broadcast([P, E, T]),
                                     pos[:, t, :, None].to_broadcast([P, E, T]), ALU.is_equal)

        def rows_by_slot(chain, layer):
            by = scr[layer]["by_slot"]
            chain.step(nc.vector.scalar_tensor_tensor(out=by[:, :, 0], in0=by[:, :, 2], scalar=no_row[:, 1:2],
                                                      in1=by[:, :, 0], op0=ALU.mult, op1=ALU.add))
            return nc.vector.scalar_tensor_tensor(out=idx[:, :], in0=by[:, :, 0], scalar=no_row[:, 0:1],
                                                  in1=by[:, :, 1], op0=ALU.add, op1=ALU.add)

        def gates_of_slots(chain, layer):
            by = scr[layer]["by_slot"]
            chain.step(nc.vector.tensor_tensor(by[:, :, 3], by[:, :, 3], by[:, :, 4], ALU.add))
            return nc.vector.tensor_tensor(slot_gate[:, :], by[:, :, 3], by[:, :, 5], ALU.add)

        def gather(pool, half, col):
            return pool.indirect_dma_start(
                out=xg[0:T, half, :], out_offset=None, in_=x_rows[:, :],
                in_offset=bass.IndirectOffsetOnAxis(ap=idx_col[0:T, col:col + 1], axis=0),
                bounds_check=S - 1, oob_is_err=False)

        def scatter(pool, layer, src, col):
            return pool.indirect_dma_start(
                out=acc[layer][:, :], out_offset=bass.IndirectOffsetOnAxis(ap=col, axis=0),
                in_=src, in_offset=None, compute_op=ALU.add)

        def slots(banks):
            return banks.rearrange("p b (k s) -> p (b k) s", s=P)[:, :, 0:T]

        class Over:

            def __init__(self, layer):
                def s(name):
                    return sem(f"over{layer}_{name}")
                self.dve, self.pool = s("dve"), s("pool")
                self.hot, self.ids, self.idx = s("hot"), s("ids"), s("idx")
                self.xg, self.tr, self.xo = s("xg"), s("tr"), s("xo")
                self.w, self.used = [s("w0"), s("w1")], s("used")
                self.silu, self.hid, self.hT, self.hTo = s("silu"), s("hid"), s("hT"), s("hTo")
                self.yo, self.out = s("yo"), s("out")

        over = [Over(0), Over(1)]
        EP = EU // 2

        def heavy(eng, layer):
            eng.wait_ge(most_ready, layer + 1)
            return eng.value_load(most[0:1, layer:layer + 1], min_val=0, max_val=S)

        def overflow_pool(pool, layer, spare):
            o, load = over[layer], heavy(pool, layer)
            chain = Chain(pool, o.pool)

            def expert(turn, e):
                q = e + E * (turn - 1)
                src = idx[:, e:e + 1] if isinstance(e, int) else idx[:, bass.ds(e, 1)]
                chain.step(nc.gpsimd.tensor_copy(idx_col[:, 0:1], src))
                used = q * EP
                if not isinstance(e, int):
                    pool.reg_mov(spare, used)
                    used = spare
                pool.wait_ge(xrow_out[0], 16 * (layer + 1))
                gather(pool, 0, 0).then_inc(o.xg, 16)
                for k in range(EP):
                    if k >= 2:
                        pool.wait_ge(o.used, q * EP + (k - 1))
                    elif not is_zero(q):
                        pool.wait_ge(o.used, used)
                    pool.dma_start(w_over[:, k % 2, :], w_moe[layer, e, k, :, :]).then_inc(o.w[k % 2], 16)
                pool.wait_ge(o.yo, q + 1)
                over_ = (q + 1) * 16
                if not isinstance(e, int):
                    pool.reg_mov(spare, over_)
                    over_ = spare
                pool.wait_ge(y_out, 16 * E * (layer + 1))
                scatter(pool, layer, y_over[0:T, :], idx_col[0:T, 0:1]).then_inc(o.out, 16)
                pool.wait_ge(o.out, over_)

            for turn in range(1, TILES):
                with pool.If(load > T * turn):
                    pool.wait_ge(xgT_ready, E * (layer + 1))
                    pool.wait_ge(o.idx, turn)
                    pool.wait_ge(lo_ready, LO_DVE[MOE[layer] + E * EU - 1])
                    expert(turn, 0)
                    with pool.Fori(0, E - 1) as i:
                        chain.enter(i, 1)
                        expert(turn, i + 1)
                    chain.leave(E - 1)

        def overflow_dve(dve, layer):
            o, load = over[layer], heavy(dve, layer)
            chain = Chain(dve, o.dve)
            for turn in range(1, TILES):
                q0 = E * (turn - 1)
                with dve.If(load > T * turn):
                    dve.wait_ge(hT_lo_ready, E * (layer + 1))
                    dve.wait_ge(gates_done, layer + 1)
                    chain.step(nc.vector.tensor_scalar(scr[layer]["place_"][:, :, :], posm[:, :, :], float(T * turn), None,
                                                       ALU.subtract))
                    for t in range(NT):
                        if t:
                            dve.wait_ge(o.ids, NT * (turn - 1) + t)
                        slots_hot(dve, hot[layer][0], scr[layer]["place_"], t).then_inc(o.hot, 1)
                    dve.wait_ge(o.ids, NT * turn)
                    chain.step(nc.vector.tensor_copy(scr[layer]["by_slot"][:, :, :],
                                                     ps[:, 7, 0:6 * E].rearrange("p (e a) -> p e a", a=6)))
                    dve.wait_ge(y_out, 16 * E * (layer + 1))
                    dve.wait_ge(y_copied, E * (layer + 1))
                    rows_by_slot(chain, layer).then_inc(o.dve, 1)
                    chain.n += 1
                    gates_of_slots(chain, layer).then_inc(o.idx, 1)
                    with dve.Fori(0, E) as e:
                        dve.wait_ge(o.silu, e + (q0 + 1))
                        nc.vector.tensor_tensor(hid[0:T, :], sgate[0:T, :], ps[0:T, 1, :], ALU.mult).then_inc(o.hid, 1)
                    dve.wait_ge(o.out, 16 * (q0 + E))

        def overflow_act(act, layer):
            o, load = over[layer], heavy(act, layer)

            def expert(turn, e):
                q = e + E * (turn - 1)
                act.wait_ge(o.tr, q + 1)
                nc.scalar.activation(x_over[:, :, 0:T], slots(ps[:, 5:7, :]), ACT.Copy).then_inc(o.xo, 1)
                act.wait_ge(o.used, q * EP + GU // 2)
                nc.scalar.activation(sgate[0:T, :], ps[0:T, 0, :], ACT.Silu).then_inc(o.silu, 1)
                act.wait_ge(o.hT, q + 1)
                nc.scalar.activation(h_over[:, :, 0:T], slots(ps[:, 4:5, :]), ACT.Copy).then_inc(o.hTo, 1)
                act.wait_ge(o.used, q * EP + EP)
                if not is_zero(q):
                    act.wait_ge(o.out, q * 16)
                weight = slot_gate[0:T, e:e + 1] if isinstance(e, int) else slot_gate[0:T, bass.ds(e, 1)]
                nc.scalar.activation(y_over[0:T, :], ps[0:T, 2:4, :].rearrange("p b n -> p (b n)"), ACT.Copy,
                                     scale=weight).then_inc(o.yo, 1)

            for turn in range(1, TILES):
                with act.If(load > T * turn):
                    expert(turn, 0)
                    with act.Fori(0, E - 1) as i:
                        expert(turn, i + 1)
                    act.wait_ge(o.out, 16 * E * turn)

        def overflow_pe(pe, layer, sum_by_slot):
            o, load = over[layer], heavy(pe, layer)

            def expert(turn, e):
                q = e + E * (turn - 1)
                pe.wait_ge(o.xg, q * 16 + 16)
                for k in range(KD):
                    ins = nc.tensor.transpose(ps[:, 5 + k // 4, (k % 4) * P:(k % 4) * P + T],
                                              xg[0:T, 0, k * P:(k + 1) * P], ident[0:T, 0:T])
                ins.then_inc(o.tr, 1)
                pe.wait_ge(o.xo, q + 1)
                for k in range(EP):
                    if k == GU // 2:
                        pe.wait_ge(o.hid, q + 1)
                        for f in range(KF):
                            ins = nc.tensor.transpose(ps[:, 4, f * P:f * P + T], hid[0:T, f * P:(f + 1) * P],
                                                      ident[0:T, 0:T])
                        ins.then_inc(o.hT, 1)
                        pe.wait_ge(o.hTo, q + 1)
                        if not is_zero(q):
                            pe.wait_ge(o.yo, q)
                    pe.wait_ge(o.w[k % 2], q * (16 * EP // 2) + 16 * (k // 2 + 1))
                    for u in range(2):
                        r = 2 * k + u
                        for h in range(2):
                            cols = slice(u * UN + h * BANK, u * UN + (h + 1) * BANK)
                            if r < GU:
                                ins = nc.tensor.matmul(ps[0:T, h, :], x_over[:, r, 0:T], w_over[:, k % 2, cols],
                                                       start=(r == 0), stop=(r == GU - 1))
                            else:
                                ins = nc.tensor.matmul(ps[0:T, 2 + h, :], h_over[:, r - GU, 0:T], w_over[:, k % 2, cols],
                                                       start=(r == GU), stop=(r == EU - 1))
                    ins.then_inc(o.used, 1)

            for turn in range(1, TILES):
                with pe.If(load > T * turn):
                    for t in range(NT):
                        pe.wait_ge(o.hot, NT * (turn - 1) + t + 1)
                        sum_by_slot(hot[layer][0], 7, t, 0, 6).then_inc(o.ids, 1)
                    pe.wait_ge(y_copied, E * (layer + 1))
                    pe.wait_ge(hT_lo_ready, E * (layer + 1))
                    expert(turn, 0)
                    with pe.Fori(0, E - 1) as i:
                        expert(turn, i + 1)

        @block.sync
        def _(sp):
            counts = [sp.alloc_register("count0"), sp.alloc_register("count1")]

            def pair_of(w, c, i, k=2):
                j = plus(c, i, k)
                return w[j if isinstance(j, int) else sp.snap(j)]

            def load_pair(n, src, step=0, i=0):
                if raw_slot(n) >= RING and n - MOE[layer_of(n)] < len(RAW_ORDER):
                    sp.wait_ge(unit_used, MOE[layer_of(n)])
                if RAW_BEFORE[n] is not None:
                    m = RAW_BEFORE[n]
                    if POOL[m] != POOL[m + 1]:
                        first = lo_count(sp, m, step, i, counts[0])
                        second = lo_count(sp, m + 1, step, i, counts[1])
                        sp.wait_ge(lo_sem(m), first)
                        sp.wait_ge(lo_sem(m + 1), second)
                    else:
                        wait_lo(sp, m + 1, step, i)
                sp.dma_start(flat(raw_units(n, 2)), src).then_inc(raw_in[raw_slot(n) // 2], 16)

            for c in range(4):
                sp.dma_start(xT_raw[:, 2 * c:2 * c + 2, :].rearrange("p k s -> p (k s)"), x_t[c, :, :]) \
                  .then_inc(xt_in[c], 16)
                if c == 0:
                    load_pair(0, w_dense0[0, :, :])
            for m in (1, 2):
                load_pair(2 * m, w_dense0[m, :, :])
            with sp.Fori(0, 3) as i:
                for m in range(3):
                    load_pair(CRING + 2 * m, pair_of(w_dense0, 3 + m, i, 3), CRING, i)
            sp.dma_start(X[:, :, :], x.rearrange("(t p) d -> p t d", p=P)).then_inc(x_in, 16)
            for m in range(12, 16):
                load_pair(2 * m, w_dense0[m, :, :])

            def experts(layer):
                def expert_pair(c, i, k):
                    e = plus(c, i)
                    return w_moe[layer, e if isinstance(e, int) else sp.snap(e), k, :, :]

                def turn(e, i=0):
                    step = 0 if isinstance(i, int) else 2 * EU
                    for k in range(GU // 2):
                        load_pair(gu0(layer, e + 1) + 2 * k, expert_pair(e + 1, i, k), step, i)
                    for k in range(DN // 2):
                        load_pair(dn0(layer, e) + 2 * k, expert_pair(e, i, GU // 2 + k), step, i)

                for k in range(GU // 2):
                    load_pair(gu0(layer, 0) + 2 * k, w_moe[layer, 0, k, :, :])
                turn(0)
                turn(1)
                with sp.Fori(0, 6) as i:
                    turn(2, i)
                    turn(3, i)
                turn(14)
                for k in range(DN // 2):
                    load_pair(dn0(layer, E - 1) + 2 * k, w_moe[layer, E - 1, GU // 2 + k, :, :])

            def sums(layer):
                sp.wait_ge(acc_out, 16 * (NT + 1) * (layer + 1))
                sp.wait_ge(summed, layer + 1)
                for t in range(NT):
                    sp.dma_start(X[:, t, :], acc[layer][t * P:(t + 1) * P, :]).then_inc(acc_in[t], 16)

            experts(0)
            for k in range(4):
                load_pair(U0 + 2 * k, w_dense1[k, :, :])
            sums(0)
            with sp.Fori(0, 5) as i:
                for m in range(4):
                    load_pair(U0 + 8 + 2 * m, pair_of(w_dense1, 4 + m, i, 4), RING, i)
            experts(1)
            sums(1)

        @block.gpsimd
        def _(pool):
            chain = Chain(pool, pool_step)
            spare = pool.alloc_register("spare")
            for t_, v_ in ((eps, EPS), (ones_b, 1.0), (ones_f, 1.0), (warm, 1.0)):
                chain.post(nc.gpsimd.memset(t_[:, :], v_))
            chain.step(nc.gpsimd.memset(ch[:, 0:2], 0.0))
            chain.post(nc.gpsimd.affine_select(out=ident[:, :], in_=ones_f[:, :], compare_op=ALU.is_equal, fill=0.0,
                                               base=0, pattern=[[-1, P]], channel_multiplier=1))
            chain.post(nc.gpsimd.affine_select(out=tri[:, :], in_=ones_b[:, :], compare_op=ALU.is_ge, fill=0.0,
                                               base=0, pattern=[[1, P]], channel_multiplier=-1))
            chain.post(nc.gpsimd.affine_select(out=earlier[:, :, :],
                                               in_=ones_f[:, 0:G * G].rearrange("p (i j) -> p i j", i=G),
                                               compare_op=ALU.is_gt, fill=0.0,
                                               base=0, pattern=[[1, G], [-1, G]], channel_multiplier=0))
            chain.step(nc.gpsimd.iota(iota_i[:, :], pattern=[[1, P]], base=1, channel_multiplier=0))
            chain.step(nc.gpsimd.tensor_copy(iota_s[:, :], iota_i[:, :]))
            chain.step(nc.gpsimd.iota(iota_i[:, 0:NT], pattern=[[P, NT]], base=0, channel_multiplier=0))
            chain.step(nc.gpsimd.tensor_copy(tok_par[:, :, :, 0], iota_i[:, 0:NT, None].to_broadcast([P, NT, E])))
            chain.step(nc.gpsimd.iota(iota_i[:, 0:NT], pattern=[[0, NT]], base=0, channel_multiplier=1))
            chain.post(nc.gpsimd.tensor_copy(tok_par[:, :, :, 1], iota_i[:, 0:NT, None].to_broadcast([P, NT, E])))
            chain.step(nc.gpsimd.memset(tok_par[:, :, :, 2], 1.0))
            chain.step(nc.gpsimd.iota(iota_i[:, 0:1], pattern=[[0, 1]], base=S, channel_multiplier=1))
            chain.post(nc.gpsimd.tensor_copy(no_row[:, 0:1], iota_i[:, 0:1]))
            chain.step(nc.gpsimd.iota(iota_i[:, 1:2], pattern=[[0, 1]], base=-S, channel_multiplier=-1))
            nc.gpsimd.tensor_copy(no_row[:, 1:2], iota_i[:, 1:2]).then_inc(consts, 1)
            pool.wait_ge(ws_in, 16)
            nc.gpsimd.affine_select(out=bsb[:, :, :], in_=ws_sum[:, :, :], compare_op=ALU.is_ge, fill=0.0,
                                    base=0, pattern=[[0, H], [-1, P]], channel_multiplier=1).then_inc(ws_masked, 1)

            def fetch(layer, c, i=0, later=None):
                e, b, n = plus(c, i), c % 2, plus(c + E * layer, i)
                if c + E * layer >= 2:
                    pool.wait_ge(xgT_ready, n - 1)
                    pool.wait_ge(xg_in[b], plus(16 * ((c + E * layer) // 2), i, 16))
                src = idx[:, e:e + 1] if isinstance(e, int) else idx[:, bass.ds(e, 1)]
                chain.step(nc.gpsimd.tensor_copy(idx_col[:, b:b + 1], src))
                if later is not None:
                    pool.reg_mov(spare, later)
                pool.wait_ge(xrow_out[0], 16 * (layer + 1))
                gather(pool, b, b).then_inc(xg_in[b], 16)

            def add_out(layer, c, i=0, later=None):
                e, n = plus(c, i), plus(c + E * layer, i)
                pool.wait_ge(y_copied, n + 1)
                if not is_zero(n):
                    pool.wait_ge(y_out, n * 16)
                src = idx[:, e:e + 1] if isinstance(e, int) else idx[:, bass.ds(e, 1)]
                chain.step(nc.gpsimd.tensor_copy(out_col[:, :], src))
                if later is not None:
                    pool.reg_mov(spare, later)
                pool.wait_ge(acc_out, 16 * (NT + 1) * (layer + 1))
                scatter(pool, layer, y[0:T, c % 2, :], out_col[0:T, :]).then_inc(y_out, 16)

            def experts(layer):
                for k in range(GU):
                    if POOL[gu0(layer, 0) + k]:
                        split_lo(pool, gu0(layer, 0) + k)
                for t in range(NT):
                    pool.wait_ge(xrow_out[t], 16 * (layer + 1))
                pool.wait_ge(idx_ready, layer + 1)
                for e in range(3):
                    fetch(layer, e)

                def turn(e, i=0):
                    g, d = gu0(layer, e + 1) + 3, dn0(layer, e) + 3
                    if isinstance(i, int):
                        if e + 3 < E:
                            fetch(layer, e + 3)
                        split_lo(pool, g)
                        if e:
                            add_out(layer, e - 1)
                        split_lo(pool, d)
                    else:
                        fetch(layer, e + 3, i, later=at(INDEX, g, 2 * EU, i) + 1)
                        split_lo(pool, g, 2 * EU, i, count=spare)
                        add_out(layer, e - 1, i, later=at(INDEX, d, 2 * EU, i) + 1)
                        split_lo(pool, d, 2 * EU, i, count=spare)

                turn(0)
                with pool.Fori(0, 6) as i:
                    chain.enter(i, 4)
                    turn(1, i)
                    turn(2, i)
                chain.leave(6)
                turn(13)
                turn(14)
                split_lo(pool, dn0(layer, E - 1) + 3)
                add_out(layer, E - 2)
                add_out(layer, E - 1)

            experts(0)
            overflow_pool(pool, 0, spare)
            pool.wait_ge(acc_in[NT - 1], 16)
            pool.dma_start(bsb[:, :, :].rearrange("p h i -> p (h i)"), b_s.partition_broadcast(P)).then_inc(bs_in, 16)
            experts(1)
            overflow_pool(pool, 1, spare)

        @block.scalar
        def _(act):
            preloads = Chain(act, act_step)

            def copy(o, i_):
                return nc.scalar.activation(o, i_, ACT.Copy)

            def preload(func):
                preloads.step(nc.scalar.activation(warm[:, :], eps[:, :], func))

            for o, i_ in ((rw[:, :, :], router_w), (rbias[:, :], router_bias.partition_broadcast(P)),
                          (cw[:, :, :], conv_w), (vg[:, :], v_gain), (vb[:, :], v_bias)):
                act.dma_start(o, i_).then_inc(small_in, 16)
            for c in range(4):
                act.wait_ge(xt_in[c], 16)
                copy(xT_hi[:, 2 * c:2 * c + 2, :], xT_raw[:, 2 * c:2 * c + 2, :]).then_inc(xt_hi, 1)
                if c == 0:
                    split_hi(act, 0)
            for n in range(1, CRING):
                split_hi(act, n)
            act.dma_start(ws_sum[:, :, :], w_s).then_inc(ws_in, 16)

            def spatial_weights(dst):
                copy(dst[:, :, :].rearrange("p h i -> p (h i)"),
                     ps[:, 6:8, :].rearrange("p b n -> p (b n)")).then_inc(ws_copied, 1)

            def conv_tile(c, i, ahead):
                j = plus(c, i)
                for n in ahead[:-1]:
                    split_hi(act, n, CRING, i)
                act.wait_ge(unit_used, plus(3 * c + 3, i, 6))
                if c:
                    act.wait_ge(bz_ready, j)
                copy(cgate[:, :], ps[:, 3 * (c % 2) + 1, :]).then_inc(c_ready, 1)
                split_hi(act, ahead[-1], CRING, i)
                act.wait_ge(bz_ready, j + 1)
                copy(tile_of(bz_hi, j), z[:, :]).then_inc(bz_hi_ready, 1)

            conv_tile(0, 0, (6, 7, 8))
            act.wait_ge(ws_tr, 1)
            spatial_weights(wcT)
            conv_tile(1, 0, (9, 10, 11))
            act.wait_ge(ws_summed, 1)
            spatial_weights(ws_sum)
            with act.Fori(0, 2) as i:
                conv_tile(2, i, (12, 13, 14))
                conv_tile(3, i, (15, 16, 17))
            conv_tile(6, 0, (24, 25, 26, 27, 28))
            conv_tile(7, 0, (29, 30, 31))

            def params(layer, which, dst):
                for k in range(2):
                    act.dma_start(dst[:, k, :], ln_par[layer, which, k, :].partition_broadcast(P)).then_inc(par_in, 16)

            def root(q, t):
                act.wait_ge(var_ready, q + 1)
                nc.scalar.activation(std[:, t:t + 1], mv[:, t, 1:2], ACT.Sqrt, bias=eps[:, :]).then_inc(std_ready, 1)

            def router_in(layer, t):
                act.wait_ge(normed, 8 * layer + t + 1)
                act.dma_start(x_rows[t * P:(t + 1) * P, :], X[:, t, :]).then_inc(xrow_out[t], 16)
                for h in range(2):
                    act.wait_ge(tr_ready, TR_MIX[layer] + 2 * t + h + 1)
                    if h == 0 and t:
                        act.wait_ge(logit_ready, NT * layer + t)
                    copy(xTt[layer][:, 4 * h:4 * h + 4, :],
                         ps[:, TRB[layer] + h, :].rearrange("p (k s) -> p k s", k=4)).then_inc(tr_taken, 1)

            def scores(layer, t):
                if t < NT - 1:
                    preload(ACT.Sigmoid)
                act.wait_ge(logit_ready, NT * layer + t + 1)
                nc.scalar.activation(scr[layer]["sig"][:, :], ps[0:E, TRB[layer], 0:P], ACT.Sigmoid).then_inc(sig_ready, 1)

            def residual(layer, t):
                act.wait_ge(xrow_out[t], 16 * (layer + 1))
                act.wait_ge(normed, 8 * layer + t + 1)
                preloads.step(nc.scalar.activation(X[:, t, :], X[:, t, :], ACT.Copy, scale=ALPHA))
                act.dma_start(acc[layer][t * P:(t + 1) * P, :], X[:, t, :]).then_inc(acc_out, 16)
                if t == 0:
                    act.dma_start(acc[layer][S:S + P, :], X[:, t, :]).then_inc(acc_out, 16)

            def norm_and_route(layer):
                def ahead(first, n):
                    for k in range(first, first + n):
                        split_hi(act, gu0(layer, 0) + k)

                preload(ACT.Sqrt)
                root(8 * layer, 0)
                router_in(layer, 0)
                scores(layer, 0)
                preload(ACT.Sqrt)
                root(8 * layer + 1, 1)
                router_in(layer, 1)
                preload(ACT.Sqrt)
                root(8 * layer + 2, 2)
                scores(layer, 1)
                residual(layer, 0)
                router_in(layer, 2)
                residual(layer, 1)
                ahead(0, 2)
                scores(layer, 2)
                preload(ACT.Sqrt)
                ahead(2, 1)
                root(8 * layer + 3, 3)
                ahead(3, 2)
                router_in(layer, 3)
                preload(ACT.Sigmoid)
                residual(layer, 2)
                scores(layer, 3)
                ahead(5, 3)

            def experts(layer):
                m0 = E * layer

                def x_hi(c, i=0):
                    act.wait_ge(xgT_ready, plus(c + m0 + 1, i))
                    copy(xgT_hi[:, :, 0:T], slots(ps[:, 5:7, :])).then_inc(xgT_hi_ready, 1)

                def silu(c, step=0, i=0):
                    act.wait_ge(unit_used, at(INDEX, gu0(layer, c) + GU - 1, step, i) + 1)
                    if c + m0:
                        act.wait_ge(hid_ready, plus(c + m0, i))
                    nc.scalar.activation(sgate[0:T, :], ps[0:T, 0, :], ACT.Silu).then_inc(silu_ready, 1)

                def h_hi(c, i=0):
                    act.wait_ge(hT_ready, plus(c + m0 + 1, i))
                    copy(hT_hi[:, :, 0:T], slots(ps[:, 4:5, :])).then_inc(hT_hi_ready, 1)

                def y_copy(c, step=0, i=0):
                    act.wait_ge(unit_used, at(INDEX, dn0(layer, c) + DN - 1, step, i) + 1)
                    e, n = plus(c, i), plus(c + m0 - 1, i)
                    if c + m0 >= 2:
                        act.wait_ge(y_out, n * 16)
                    if c == 0:
                        act.wait_ge(slot_gate_ready, layer + 1)
                    weight = slot_gate[0:T, e:e + 1] if isinstance(e, int) else slot_gate[0:T, bass.ds(e, 1)]
                    nc.scalar.activation(y[0:T, c % 2, :], ps[0:T, 2:4, :].rearrange("p b n -> p (b n)"), ACT.Copy,
                                         scale=weight).then_inc(y_copied, 1)

                def turn(e, i=0, more_x=True):
                    step = 0 if isinstance(i, int) else 2 * EU
                    n0 = gu0(layer, e + 1) + GU
                    for k in range(GU - 1):
                        split_hi(act, n0 + k, step, i)
                    silu(e + 1, step, i)
                    if more_x:
                        x_hi(e + 2, i)
                    for k in range(GU - 1, EU):
                        if n0 + k < UNITS:
                            split_hi(act, n0 + k, step, i)
                    y_copy(e, step, i)
                    h_hi(e + 1, i)

                preload(ACT.Silu)
                x_hi(0)
                residual(layer, 3)
                for k in range(GU - 1):
                    split_hi(act, gu0(layer, 1) + k)
                silu(0)
                x_hi(1)
                split_hi(act, gu0(layer, 1) + GU - 1)
                h_hi(0)
                turn(0)
                params(layer, 1, ffn_par[layer])
                turn(1)
                with act.Fori(0, 6) as i:
                    turn(2, i)
                    turn(3, i)
                turn(14, more_x=False)
                y_copy(15)
                if layer == 0:
                    for k in range(4):
                        split_hi(act, U0 + 4 + k)

            def finish(layer, t):
                act.wait_ge(normed, 8 * layer + 4 + t + 1)
                if layer == 1:
                    act.dma_start(out[t * P:(t + 1) * P, :], X[:, t, :]).then_inc(out_done, 16)
                    return
                act.dma_start(x_mid[t * P:(t + 1) * P, :], X[:, t, :]).then_inc(xmid_out, 16)
                for h in range(2):
                    act.wait_ge(tr_ready, TR_FFN + 2 * t + h + 1)
                    copy(xT_hi[:, 4 * h:4 * h + 4, t * P:(t + 1) * P],
                         ps[:, TRF[t] + h, :].rearrange("p (k s) -> p k s", k=4)).then_inc(xt_hi, 1)

            def combine(layer):
                preload(ACT.Sqrt)
                act.wait_ge(y_out, 16 * E * (layer + 1))
                nc.scalar.activation(warm[:, :], eps[:, :], ACT.Copy).then_inc(summed, 1)
                root(8 * layer + 4, 0)
                for t in range(NT):
                    if t in (0, 2) or layer == 1 and t + 1 < NT:
                        root(8 * layer + 4 + t + 1, t + 1)
                    finish(layer, t)
                    if layer == 0 and t == 1:
                        root(8 * layer + 4 + 2, 2)

            params(0, 0, mix_par[0])
            norm_and_route(0)
            experts(0)
            overflow_act(act, 0)
            combine(0)

            preload(ACT.Gelu)
            with act.Fori(0, 2) as i:
                for a in range(8):
                    act.wait_ge(unit_used, plus(U0 + a + 1, i, 8))
                    nc.scalar.activation(tile_of(U, plus(a, i, 8)), ps[:, UB[a], :], ACT.Gelu).then_inc(u_copied, 1)
                    split_hi(act, U0 + 8 + a, RING, i)
            act.wait_ge(xmid_out, 16 * NT)
            for nb in range(4):
                for t in range(NT):
                    if t < NT - 1:
                        act.wait_ge(v_ready, (NT - 1) * nb + t + 1)
                    else:
                        act.wait_ge(unit_used, V0 + 4 * nb + 4)
                    nc.scalar.activation(V[:, 4 * nb:4 * nb + 4, t, :],
                                         ps[:, (nb % 2) * 4 + t, :].rearrange("p (j c) -> p j c", j=4),
                                         ACT.Gelu).then_inc(v_copied, 1)
                if nb < 3:
                    for k in range(4):
                        split_hi(act, V0 + 8 + 4 * nb + k)
            preload(ACT.Sqrt)
            act.wait_ge(v_stats, 1)
            nc.scalar.activation(std[:, :], mv[:, :, 1], ACT.Sqrt, bias=eps[:, :]).then_inc(v_root, 1)
            act.wait_ge(v_stats, 2)
            for js in V_PARTS:
                for t in (2, 3):
                    nc.scalar.activation(V[:, js, t, :], V[:, js, t, :], ACT.Identity, scale=rstd[:, t:t + 1],
                                         bias=nmr[:, t:t + 1]).then_inc(v_normed_a, 1)
            for j in range(NC):
                act.wait_ge(g_ready, j + 1)
                copy(gated(j)[0], U[:, j, :]).then_inc(g_hi_ready, 1)
                if j % 2:
                    split_hi(act, SO0 + 4 + (j - 1) // 2)
            act.dma_start(X[:, :, :], x_mid.ap().rearrange("(t p) d -> p t d", p=P)).then_inc(x_back, 16)
            act.wait_ge(g_lo_ready, NC)
            params(1, 0, mix_par[1])
            for n in range(12, 16):
                split_hi(act, SO0 + n)

            norm_and_route(1)
            experts(1)
            overflow_act(act, 1)
            combine(1)
            act.wait_ge(out_done, 16 * NT)

        @block.vector
        def _(dve):
            chain = Chain(dve, dve_step)

            def own_lo(n, step=0, i=0):
                if not POOL[n]:
                    split_lo(dve, n, step, i)

            for c in range(4):
                dve.wait_ge(xt_hi, c + 1)
                nc.vector.tensor_tensor(xT_lo[:, 2 * c:2 * c + 2, :], xT_raw[:, 2 * c:2 * c + 2, :],
                                        xT_hi[:, 2 * c:2 * c + 2, :], ALU.subtract).then_inc(xt_lo, 1)
                if c == 0:
                    own_lo(0)
            for n in range(1, CRING):
                own_lo(n)
            dve.wait_ge(small_in, 16 * 5)
            dve.wait_ge(consts, 1)
            dve.wait_ge(xt_lo, 4)

            def conv_tile(c, i, ahead):
                j = plus(c, i)
                for n in ahead[:-1]:
                    own_lo(n, CRING, i)
                dve.wait_ge(c_ready, j + 1)
                if c:
                    dve.wait_ge(bz_lo_ready, j)
                bank = 3 * (c % 2)
                chain.step(nc.vector.tensor_tensor(ch[:, 2:2 + S], cgate[:, :], ps[:, bank + 2, :], ALU.mult))
                tap = lambda k: cw[:, j:j + 1, k] if isinstance(j, int) else cw[:, bass.ds(j, 1), k]
                chain.step(nc.vector.tensor_scalar(z[:, :], ch[:, 2:2 + S], tap(2), None, ALU.mult))
                for k in (1, 0):
                    chain.step(nc.vector.scalar_tensor_tensor(out=z[:, :], in0=ch[:, k:k + S], scalar=tap(k),
                                                              in1=z[:, :], op0=ALU.mult, op1=ALU.add))
                nc.vector.tensor_tensor(z[:, :], z[:, :], ps[:, bank, :], ALU.mult).then_inc(bz_ready, 1)
                own_lo(ahead[-1], CRING, i)
                dve.wait_ge(bz_hi_ready, j + 1)
                nc.vector.tensor_tensor(tile_of(bz_lo, j), z[:, :], tile_of(bz_hi, j), ALU.subtract) \
                         .then_inc(bz_lo_ready, 1)

            conv_tile(0, 0, (6, 7, 8))
            conv_tile(1, 0, (9, 10, 11))
            with dve.Fori(0, 2) as i:
                chain.enter(i, 8)
                conv_tile(2, i, (12, 13, 14))
                conv_tile(3, i, (15, 16, 17))
            chain.leave(2)
            conv_tile(6, 0, (24, 25, 26, 27, 28))
            conv_tile(7, 0, (29, 30, 31))

            def moments(q, t):
                for h in range(2):
                    chain.post(nc.vector.bn_stats(stats[:, h, :], X[:, t, h * BANK:(h + 1) * BANK]))
                chain.sync()
                nc.vector.bn_aggr(mv[:, t, :], stats[:, :, :].rearrange("p a b -> p (a b)")).then_inc(var_ready, 1)
                dve.wait_ge(var_ready, q + 1)

            def norm(q, t, par, n_par):
                dve.wait_ge(par_in, 32 * n_par)
                chain.step(nc.vector.scalar_tensor_tensor(out=X[:, t, :], in0=X[:, t, :], scalar=mv[:, t, 0:1],
                                                          in1=par[:, 0, :], op0=ALU.subtract, op1=ALU.mult))
                dve.wait_ge(std_ready, q + 1)
                chain.step(nc.vector.reciprocal(rstd[:, t:t + 1], std[:, t:t + 1]))
                nc.vector.scalar_tensor_tensor(out=X[:, t, :], in0=X[:, t, :], scalar=rstd[:, t:t + 1],
                                               in1=par[:, 1, :], op0=ALU.mult, op1=ALU.add).then_inc(normed, 1)

            def mix_norm(layer, t):
                if t < NT - 1:
                    dve.wait_ge(mix_ready, (NT - 1) * layer + t + 1)
                else:
                    dve.wait_ge(unit_used, gu0(layer, 0))
                if layer == 0:
                    dve.wait_ge(x_in, 16)
                    b = (6, 0)[t % 2]
                    cols, src = slice(0, D), ps[:, b:b + 2, :].rearrange("p b n -> p (b n)")
                else:
                    cols, src = slice(BANK, D), ps[:, 4 + t, :]
                nc.vector.scalar_tensor_tensor(out=X[:, t, cols], in0=X[:, t, cols], scalar=ALPHA, in1=src,
                                               op0=ALU.mult, op1=ALU.add).then_inc(mix_taken, 1)
                dve.wait_ge(mix_taken, NT * layer + t + 1)
                moments(8 * layer + t, t)
                norm(8 * layer + t, t, mix_par[layer], 1 + 2 * layer)

            def route(layer, t):
                dve.wait_ge(s_ready, NT * layer + t + 1)
                src = ps[:, LGB[layer], P:P + E]
                chain.post(nc.vector.tensor_copy(score[:, t, :], src))
                chain.step(nc.vector.tensor_tensor(scr[layer]["biased"][:, :], src, rbias[:, :], ALU.add))
                by_g = scr[layer]["biased"][:, :].rearrange("p (g i) -> p g i", g=G)
                other = by_g[:, :, None, :].to_broadcast([P, G, G, G])
                mine = by_g[:, :, :, None].to_broadcast([P, G, G, G])
                chain.post(nc.vector.tensor_tensor(scr[layer]["beats"][:, :, :, 0, :], other, mine, ALU.is_gt))
                chain.step(nc.vector.tensor_tensor(scr[layer]["beats"][:, :, :, 1, :], other, mine, ALU.is_equal))
                chain.step(nc.vector.tensor_tensor(scr[layer]["beats"][:, :, :, 1, :], scr[layer]["beats"][:, :, :, 1, :],
                                                   earlier[:, None, :, :].to_broadcast([P, G, G, G]), ALU.mult))
                chain.step(nc.vector.reduce_sum(scr[layer]["rank"][:, :], scr[layer]["beats"][:, :, :, :, :].rearrange("p g i a j -> p (g i) (a j)"),
                                                axis=AX.X))
                chain.step(nc.vector.scalar_tensor_tensor(out=scr[layer]["top2"][:, :], in0=scr[layer]["rank"][:, :], scalar=2.0, in1=scr[layer]["biased"][:, :],
                                                          op0=ALU.is_lt, op1=ALU.mult))
                chain.step(nc.vector.reduce_sum(scr[layer]["gsc"][:, :], scr[layer]["top2"][:, :].rearrange("p (g i) -> p g i", g=G), axis=AX.X))
                other = scr[layer]["gsc"][:, None, :].to_broadcast([P, G, G])
                mine = scr[layer]["gsc"][:, :, None].to_broadcast([P, G, G])
                chain.post(nc.vector.tensor_tensor(scr[layer]["gbeats"][:, :, 0, :], other, mine, ALU.is_gt))
                chain.step(nc.vector.tensor_tensor(scr[layer]["gbeats"][:, :, 1, :], other, mine, ALU.is_equal))
                chain.step(nc.vector.tensor_tensor(scr[layer]["gbeats"][:, :, 1, :], scr[layer]["gbeats"][:, :, 1, :], earlier[:, :, :], ALU.mult))
                chain.step(nc.vector.reduce_sum(scr[layer]["grank"][:, :], scr[layer]["gbeats"][:, :, :, :].rearrange("p i a j -> p i (a j)"), axis=AX.X))
                chain.step(nc.vector.scalar_tensor_tensor(out=order[:, t, :].rearrange("p (g i) -> p g i", g=G),
                                                          in0=scr[layer]["grank"][:, :, None].to_broadcast([P, G, G]), scalar=4.0,
                                                          in1=scr[layer]["rank"][:, :].rearrange("p (g i) -> p g i", g=G),
                                                          op0=ALU.mult, op1=ALU.add))
                nc.vector.tensor_scalar(sel[:, t, :], order[:, t, :], 2.0, None, ALU.is_lt).then_inc(sel_ready, 1)
                dve.wait_ge(pos_ready, NT * layer + t + 1)
                chain.step(nc.vector.tensor_tensor(posm[:, t, :], sel[:, t, :], ps[:, LGB[layer], 160:160 + E], ALU.mult))
                slots_hot(dve, hot[layer][t], posm, t).then_inc(hot_ready, 1)

            def route_ids(layer):
                dve.wait_ge(ids_ready, NT * layer + NT)
                chain.step(nc.vector.tensor_copy(scr[layer]["by_slot"][:, :, 0:3],
                                                 ps[:, IDB[layer], 0:3 * E].rearrange("p (e a) -> p e a", a=3)))
                rows_by_slot(chain, layer).then_inc(idx_ready, 1)

            def route_gates(layer):
                dve.wait_ge(cnt_ready, layer + 1)
                chain.step(nc.vector.reduce_max(scr[layer]["most_f"][:, :], ps[:, LGB[layer], 192:192 + E], axis=AX.X))
                nc.vector.tensor_copy(most[:, layer:layer + 1], scr[layer]["most_f"][:, :]).then_inc(most_ready, 1)
                gates, gsum = scr[layer]["gates"], scr[layer]["gsum"]
                chain.step(nc.vector.tensor_tensor(gates[:, :, :], score[:, :, :], sel[:, :, :], ALU.mult))
                chain.step(nc.vector.reduce_sum(gsum[:, :], gates[:, :, :], axis=AX.X))
                chain.step(nc.vector.reciprocal(gsum[:, :], gsum[:, :]))
                chain.step(nc.vector.tensor_tensor(gates[:, :, :], gates[:, :, :],
                                                   gsum[:, :, None].to_broadcast([P, NT, E]), ALU.mult))
                for part in (3, 4):
                    chain.step(nc.vector.tensor_copy(tok_par[:, :, :, part], gates[:, :, :]))
                    chain.step(nc.vector.tensor_tensor(gates[:, :, :], gates[:, :, :], tok_par[:, :, :, part], ALU.subtract))
                nc.vector.tensor_copy(tok_par[:, :, :, 5], gates[:, :, :]).then_inc(gates_done, 1)

            def slot_gates(layer):
                dve.wait_ge(gates_by_slot, layer + 1)
                chain.step(nc.vector.tensor_copy(scr[layer]["by_slot"][:, :, 3:6],
                                                 ps[:, 7, 0:3 * E].rearrange("p (e a) -> p e a", a=3)))
                gates_of_slots(chain, layer).then_inc(slot_gate_ready, 1)

            def norm_and_route(layer):
                mix_norm(layer, 0)
                for t in range(1, NT):
                    mix_norm(layer, t)
                    route(layer, t - 1)
                route(layer, NT - 1)
                route_ids(layer)
                own_lo(gu0(layer, 0) + GU - 1)

            def experts(layer):
                m0 = E * layer

                def x_lo(c, i=0):
                    dve.wait_ge(xgT_hi_ready, plus(c + m0 + 1, i))
                    nc.vector.tensor_tensor(xgT_lo[:, :, 0:T], slots(ps[:, 5:7, :]), xgT_hi[:, :, 0:T], ALU.subtract) \
                             .then_inc(xgT_lo_ready, 1)

                def hidden(c, i=0):
                    dve.wait_ge(silu_ready, plus(c + m0 + 1, i))
                    if c + m0:
                        dve.wait_ge(hT_ready, plus(c + m0, i))
                    nc.vector.tensor_tensor(hid[0:T, :], sgate[0:T, :], ps[0:T, 1, :], ALU.mult).then_inc(hid_ready, 1)

                def h_lo(c, i=0):
                    dve.wait_ge(hT_hi_ready, plus(c + m0 + 1, i))
                    nc.vector.tensor_tensor(hT_lo[:, :, 0:T], slots(ps[:, 4:5, :]), hT_hi[:, :, 0:T], ALU.subtract) \
                             .then_inc(hT_lo_ready, 1)

                def turn(e, i=0, more_x=True, gates=False):
                    step = 0 if isinstance(i, int) else 2 * EU
                    n0 = gu0(layer, e + 1) + GU
                    for k in range(GU - 1):
                        own_lo(n0 + k, step, i)
                    hidden(e + 1, i)
                    if gates:
                        slot_gates(layer)
                    if more_x:
                        x_lo(e + 2, i)
                    for k in range(GU - 1, EU):
                        if n0 + k < UNITS:
                            own_lo(n0 + k, step, i)
                    h_lo(e + 1, i)

                x_lo(0)
                route_gates(layer)
                for k in range(GU - 1):
                    own_lo(gu0(layer, 1) + k)
                hidden(0)
                x_lo(1)
                own_lo(gu0(layer, 1) + GU - 1)
                h_lo(0)
                turn(0, gates=True)
                turn(1)
                with dve.Fori(0, 6) as i:
                    turn(2, i)
                    turn(3, i)
                turn(14, more_x=False)
                if layer == 0:
                    for k in range(4):
                        own_lo(U0 + 4 + k)

            def combine(layer):
                def x_lo(t):
                    for h in range(2):
                        dve.wait_ge(xt_hi, 4 + 2 * t + h + 1)
                        dst = slice(4 * h, 4 * h + 4), slice(t * P, (t + 1) * P)
                        nc.vector.tensor_tensor(xT_lo[:, dst[0], dst[1]],
                                                ps[:, TRF[t] + h, :].rearrange("p (k s) -> p k s", k=4),
                                                xT_hi[:, dst[0], dst[1]], ALU.subtract).then_inc(xt_lo, 1)

                def first(t):
                    dve.wait_ge(acc_in[t], 16 * (layer + 1))
                    moments(8 * layer + 4 + t, t)

                def second(t):
                    norm(8 * layer + 4 + t, t, ffn_par[layer], 2 + 2 * layer)

                first(0)
                if layer == 1:
                    first(1)
                    for t in range(NT):
                        second(t)
                        if t + 2 < NT:
                            first(t + 2)
                else:
                    second(0)
                    first(1)
                    second(1)
                    x_lo(0)
                    first(2)
                    x_lo(1)
                    second(2)
                    first(3)
                    second(3)
                    x_lo(2)
                    x_lo(3)

            norm_and_route(0)
            experts(0)
            overflow_dve(dve, 0)
            combine(0)

            with dve.Fori(0, 2) as i:
                for a in range(8):
                    own_lo(U0 + 8 + a, RING, i)
            for nb in range(4):
                for t in range(NT):
                    dve.wait_ge(v_copied, NT * nb + t + 1)
                    chain.post(nc.vector.bn_stats(v_parts[:, t, nb, :], V[:, 4 * nb:4 * nb + 4, t, :]))
                for k in range(4):
                    if nb < 3:
                        own_lo(V0 + 8 + 4 * nb + k)
            chain.sync()
            for t in range(NT):
                ins = nc.vector.bn_aggr(mv[:, t, :], v_parts[:, t, :, :].rearrange("p a b -> p (a b)"))
                if t < NT - 1:
                    chain.post(ins)
            ins.then_inc(v_stats, 1)
            dve.wait_ge(v_root, 1)
            chain.step(nc.vector.reciprocal(rstd[:, :], std[:, :]))
            nc.vector.scalar_tensor_tensor(out=nmr[:, :], in0=mv[:, :, 0], scalar=-1.0, in1=rstd[:, :],
                                           op0=ALU.mult, op1=ALU.mult).then_inc(v_stats, 1)
            for js in V_PARTS:
                for t in (0, 1):
                    nc.vector.tensor_scalar(V[:, js, t, :], V[:, js, t, :], mv[:, t, 0:1], rstd[:, t:t + 1],
                                            ALU.subtract, ALU.mult).then_inc(v_normed, 1)
            dve.wait_ge(bs_in, 16)
            dve.wait_ge(ws_copied, 2)

            def g_lo(j):
                dve.wait_ge(g_hi_ready, j + 1)
                nc.vector.tensor_tensor(gated(j)[1], U[:, j, :], gated(j)[0], ALU.subtract).then_inc(g_lo_ready, 1)

            for j in range(NC):
                h = j // 2
                chain.step(nc.vector.scalar_tensor_tensor(out=rank1[:, :], in0=ws_sum[:, h, :], scalar=vb[:, j:j + 1],
                                                          in1=bsb[:, h, :], op0=ALU.mult, op1=ALU.add))
                dve.wait_ge(sg_ready, j + 1)
                nc.vector.scalar_tensor_tensor(out=V[:, j, :, :], in0=ps[:, 4 + j % 4, :].rearrange("p (t i) -> p t i", t=NT),
                                               scalar=vg[:, j:j + 1],
                                               in1=rank1[:, None, :].to_broadcast([P, NT, P]),
                                               op0=ALU.mult, op1=ALU.add).then_inc(sg_taken, 1)
                dve.wait_ge(sg_taken, j + 1)
                nc.vector.tensor_tensor(U[:, j, :], U[:, j, :], V[:, j, :, :].rearrange("p t i -> p (t i)"), ALU.mult) \
                         .then_inc(g_ready, 1)
                if j:
                    g_lo(j - 1)
                if j >= 2 and j % 2 == 0:
                    own_lo(SO0 + 4 + (j - 2) // 2)
            g_lo(NC - 1)
            for n in range(11, 16):
                own_lo(SO0 + n)
            dve.wait_ge(x_back, 16)
            dve.wait_ge(unit_used, SO0 + 8)
            for t in range(NT):
                nc.vector.scalar_tensor_tensor(out=X[:, t, 0:BANK], in0=X[:, t, 0:BANK], scalar=ALPHA, in1=ps[:, t, :],
                                               op0=ALU.mult, op1=ALU.add).then_inc(nh0_taken, 1)
            dve.wait_ge(nh0_taken, NT)

            norm_and_route(1)
            experts(1)
            overflow_dve(dve, 1)
            combine(1)

        @block.tensor
        def _(pe):
            def conv_tile(c, i=0):
                j = plus(c, i)
                if c >= 2:
                    pe.wait_ge(bz_ready, j - 1)
                for g in range(3):
                    n = 3 * c + g
                    s = slot_of(n)
                    wait_lo(pe, n, CRING, i)
                    for k in range(KD):
                        if c == 0 and g == 0 and k % 2 == 0:
                            pe.wait_ge(xt_lo, k // 2 + 1)
                        w = slice(k * P, (k + 1) * P)
                        ins = passes(ps[:, 3 * (c % 2) + g, :], hi[:, s, w], lo[:, s, w], xT_hi[:, k, :], xT_lo[:, k, :],
                                     k == 0, k == KD - 1)
                    ins.then_inc(unit_used, 1)

            conv_tile(0)
            pe.wait_ge(consts, 1)
            pe.wait_ge(ws_masked, 1)
            for h in range(H):
                ins = nc.tensor.transpose(ps[:, 6 + h // 4, (h % 4) * P:(h % 4 + 1) * P], bsb[:, h, :], ident[:, :])
            ins.then_inc(ws_tr, 1)
            conv_tile(1)
            pe.wait_ge(ws_copied, 1)
            for b in range(2):
                ins = nc.tensor.matmul(ps[:, 6 + b, :], ones_f[:, :], wcT[:, 4 * b:4 * b + 4, :].rearrange("p h i -> p (h i)"),
                                       start=True, stop=True)
            ins.then_inc(ws_summed, 1)
            with pe.Fori(0, 3) as i:
                conv_tile(2, i)
                conv_tile(3, i)
            pe.wait_ge(ws_copied, 2)

            def mix(layer, t, between):
                if layer == 0:
                    steps = [(k, h, OUT0 + k) for k in range(KD) for h in range(2)]
                else:
                    steps = [(k, 0, SO0 + 8 + k // 2) for k in range(NC)]
                tok = slice(t * P, (t + 1) * P)
                for m, (k, h, n) in enumerate(steps):
                    s = slot_of(n)
                    if layer == 0:
                        if t == 0 and h == 0:
                            pe.wait_ge(bz_lo_ready, k + 1)
                            wait_lo(pe, n)
                        if t == 1 and m == 0:
                            pe.wait_ge(bz_ready, KD)
                        if t > 1 and m == 0:
                            pe.wait_ge(mix_taken, t - 1)
                        a_hi, a_lo = bz_hi[:, k, tok], bz_lo[:, k, tok]
                        cols, bank = slice(h * BANK, (h + 1) * BANK), (6, 0)[t % 2] + h
                        last_of_unit = h == 1
                        first, last = k == 0, k == KD - 1
                    else:
                        if t == 0 and k % 2 == 0:
                            wait_lo(pe, n)
                        a_hi, a_lo = (part[:, tok] for part in gated(k))
                        cols, bank = slice((k % 2) * BANK, (k % 2 + 1) * BANK), 4 + t
                        last_of_unit = k % 2 == 1
                        first, last = k == 0, k == NC - 1
                    ins = passes(ps[:, bank, :], a_hi, a_lo, hi[:, s, cols], lo[:, s, cols], first, last)
                    if t == NT - 1 and last_of_unit:
                        ins.then_inc(unit_used, 1)
                    elif t < NT - 1 and m == len(steps) - 1:
                        ins.then_inc(mix_ready, 1)
                    if m % 4 == 3:
                        for f in between.get(m // 4, ()):
                            f()

            def turn_tile(q, t, bank):
                pe.wait_ge(normed, q + 1)
                for h in range(2):
                    for k in range(4):
                        ins = nc.tensor.transpose(ps[:, bank + h, k * P:(k + 1) * P],
                                                  X[:, t, (4 * h + k) * P:(4 * h + k + 1) * P], ident[:, :])
                    ins.then_inc(tr_ready, 1)

            def logits(layer, t):
                pe.wait_ge(tr_taken, 8 * layer + 2 * t + 2)
                for k in range(KD):
                    ins = nc.tensor.matmul(ps[0:E, TRB[layer], 0:P], rw[:, k, :], xTt[layer][:, k, :],
                                           start=(k == 0), stop=(k == KD - 1))
                ins.then_inc(logit_ready, 1)

            def by_token(layer, t):
                pe.wait_ge(sig_ready, NT * layer + t + 1)
                nc.tensor.transpose(ps[:, LGB[layer], P:P + E], scr[layer]["sig"][:, :], ident[0:E, 0:E]).then_inc(s_ready, 1)

            def positions(layer, t):
                pe.wait_ge(sel_ready, NT * layer + t + 1)
                dst = ps[:, LGB[layer], 160:160 + E]
                for u in range(t):
                    nc.tensor.matmul(dst, ones_b[:, :], sel[:, u, :], start=(u == 0), stop=False)
                nc.tensor.matmul(dst, tri[:, :], sel[:, t, :], start=(t == 0), stop=True).then_inc(pos_ready, 1)

            def ids(layer, t):
                pe.wait_ge(hot_ready, NT * layer + t + 1)
                sum_by_slot(hot[layer][t], IDB[layer], t, 0, 3).then_inc(ids_ready, 1)

            def sum_by_slot(onehot, bank, t, first, n):
                for e in range(E):
                    ins = nc.tensor.matmul(ps[0:T, bank, n * e:n * (e + 1)], onehot[:, e, :],
                                           tok_par[:, t, e, first:first + n],
                                           start=(t == 0 and e == 0), stop=(t == NT - 1), skip_group_check=True)
                return ins

            def gates_to_slots(layer):
                pe.wait_ge(gates_done, layer + 1)
                for t in range(NT):
                    ins = sum_by_slot(hot[layer][t], 7, t, 3, 3)
                ins.then_inc(gates_by_slot, 1)

            def mix_and_route(layer):
                T = lambda t: lambda: turn_tile(8 * layer + t, t, TRB[layer])
                L = lambda t: lambda: logits(layer, t)
                B = lambda t: lambda: by_token(layer, t)
                C = lambda t: lambda: positions(layer, t)
                I = lambda t: lambda: ids(layer, t)
                mix(layer, 0, {})
                mix(layer, 1, {2: (T(0),), 3: (L(0),)})
                mix(layer, 2, {0: (B(0),), 2: (T(1),), 3: (C(0),)})
                mix(layer, 3, {0: (I(0), L(1)), 1: (B(1),), 2: (T(2),), 3: (C(1), L(2))})
                for f in (I(1), B(2), T(3), C(2), L(3), I(2), B(3), C(3), I(3)):
                    f()
                for u in range(NT):
                    ins = nc.tensor.matmul(ps[:, LGB[layer], 192:192 + E], ones_b[:, :], sel[:, u, :],
                                           start=(u == 0), stop=(u == NT - 1))
                ins.then_inc(cnt_ready, 1)

            def experts(layer):
                m0 = E * layer

                def turn_x(c, i=0):
                    pe.wait_ge(xg_in[c % 2], plus(16 * ((c + m0) // 2 + 1), i, 16))
                    if c + m0:
                        pe.wait_ge(xgT_lo_ready, plus(c + m0, i))
                    for k in range(KD):
                        ins = nc.tensor.transpose(ps[:, 5 + k // 4, (k % 4) * P:(k % 4) * P + T],
                                                  xg[0:T, c % 2, k * P:(k + 1) * P], ident[0:T, 0:T])
                    ins.then_inc(xgT_ready, 1)

                def gate_up(c, step=0, i=0):
                    pe.wait_ge(xgT_lo_ready, plus(c + m0 + 1, i))
                    if c + m0:
                        pe.wait_ge(hid_ready, plus(c + m0, i))
                    for k in range(GU):
                        n = gu0(layer, c) + k
                        s = slot_of(n)
                        wait_lo(pe, n, step, i)
                        for h in range(2):
                            cols = slice(h * F, (h + 1) * F)
                            ins = passes(ps[0:T, h, :], xgT_hi[:, k, 0:T], xgT_lo[:, k, 0:T], hi[:, s, cols], lo[:, s, cols],
                                         k == 0, k == GU - 1)
                        ins.then_inc(unit_used, 1)

                def turn_h(c, i=0):
                    pe.wait_ge(hid_ready, plus(c + m0 + 1, i))
                    if c + m0:
                        pe.wait_ge(hT_lo_ready, plus(c + m0, i))
                    for k in range(KF):
                        ins = nc.tensor.transpose(ps[:, 4, k * P:k * P + T], hid[0:T, k * P:(k + 1) * P],
                                                  ident[0:T, 0:T])
                    ins.then_inc(hT_ready, 1)

                def down(c, step=0, i=0):
                    pe.wait_ge(hT_lo_ready, plus(c + m0 + 1, i))
                    if c + m0:
                        pe.wait_ge(y_copied, plus(c + m0, i))
                    for k in range(DN):
                        n = dn0(layer, c) + k
                        s = slot_of(n)
                        wait_lo(pe, n, step, i)
                        for h in range(2):
                            cols = slice(h * BANK, (h + 1) * BANK)
                            ins = passes(ps[0:T, 2 + h, :], hT_hi[:, k, 0:T], hT_lo[:, k, 0:T], hi[:, s, cols], lo[:, s, cols],
                                         k == 0, k == DN - 1)
                        ins.then_inc(unit_used, 1)

                def turn(e, i=0, more_x=True, gates=False):
                    step = 0 if isinstance(i, int) else 2 * EU
                    gate_up(e + 1, step, i)
                    if gates:
                        gates_to_slots(layer)
                    if more_x:
                        turn_x(e + 2, i)
                    down(e, step, i)
                    turn_h(e + 1, i)

                turn_x(0)
                gate_up(0)
                turn_x(1)
                turn_h(0)
                turn(0, gates=True)
                turn(1)
                with pe.Fori(0, 6) as i:
                    turn(2, i)
                    turn(3, i)
                turn(14, more_x=False)
                down(15)

            mix_and_route(0)
            experts(0)
            overflow_pe(pe, 0, sum_by_slot)
            def turned(t):
                if t > 1:
                    pe.wait_ge(xt_lo, 4 + 2 * t)
                turn_tile(4 + t, t, TRF[t])

            def u_tile(a, tok):
                n, s = U0 + a, slot_of(U0 + a)
                wait_lo(pe, n)
                for k in range(KD):
                    w = slice(k * P, (k + 1) * P)
                    ins = passes(ps[:, UB[a % 8], tok], hi[:, s, w], lo[:, s, w], xT_hi[:, k, tok], xT_lo[:, k, tok],
                                 k == 0, k == KD - 1)
                return ins

            turned(0)
            turned(1)
            pe.wait_ge(xt_lo, 4 + 4)
            for a in range(6):
                u_tile(a, slice(0, S // 2))
                if a in (1, 3):
                    turned((a + 3) // 2)
            pe.wait_ge(xt_lo, 4 + 2 * NT)
            for a in range(NC):
                if a >= 8:
                    pe.wait_ge(u_copied, a - 7)
                u_tile(a, slice(S // 2, S) if a < 6 else slice(0, S)).then_inc(unit_used, 1)
            for nb in range(4):
                for m in range(4):
                    n, s = V0 + 4 * nb + m, slot_of(V0 + 4 * nb + m)
                    wait_lo(pe, n)
                    for kk in range(2):
                        k = 2 * m + kk
                        for t in range(NT):
                            if k == 0:
                                if nb < 2:
                                    pe.wait_ge(u_copied, 9 + UB.index(4 * nb + t))
                                else:
                                    pe.wait_ge(v_copied, NT * (nb - 2) + t + 1)
                            tok, cols = slice(t * P, (t + 1) * P), slice(kk * BANK, (kk + 1) * BANK)
                            ins = passes(ps[:, (nb % 2) * 4 + t, :], xT_hi[:, k, tok], xT_lo[:, k, tok],
                                         hi[:, s, cols], lo[:, s, cols], k == 0, k == KD - 1)
                            if k == KD - 1 and t < NT - 1:
                                ins.then_inc(v_ready, 1)
                    ins.then_inc(unit_used, 1)

            def spatial(j):
                if j >= 4:
                    pe.wait_ge(sg_taken, j - 3)
                for t in range(NT):
                    ins = nc.tensor.matmul(ps[:, 4 + j % 4, t * P:(t + 1) * P], V[:, j, t, :], wcT[:, j // 2, :],
                                           start=True, stop=True)
                ins.then_inc(sg_ready, 1)

            pe.wait_ge(v_normed, 2)
            pe.wait_ge(v_normed_a, 2)
            for j in range(4):
                spatial(j)
            pe.wait_ge(v_normed, 4)
            pe.wait_ge(v_normed_a, 4)
            for m in range(8):
                n, s = SO0 + m, slot_of(SO0 + m)
                wait_lo(pe, n)
                for kk in range(2):
                    k = 2 * m + kk
                    pe.wait_ge(g_lo_ready, k + 1)
                    for t in range(NT):
                        tok, cols = slice(t * P, (t + 1) * P), slice(kk * BANK, (kk + 1) * BANK)
                        a_hi, a_lo = (part[:, tok] for part in gated(k))
                        ins = passes(ps[:, t, :], a_hi, a_lo, hi[:, s, cols], lo[:, s, cols], k == 0, k == NC - 1)
                    if kk == 1:
                        ins.then_inc(unit_used, 1)
                    if k + 4 < NC:
                        spatial(k + 4)
            pe.wait_ge(sg_taken, NC)
            mix_and_route(1)
            experts(1)
            overflow_pe(pe, 1, sum_by_slot)


def _pairs(units):
    n = units.shape[0] // 2
    return units.reshape(n, 2, P, UN).transpose(0, 2, 1, 3).reshape(n, P, 2 * UN)


def kernel(**inputs):
    import numpy as np
    from concourse import bacc
    from concourse.bass_utils import run_bass_kernel_spmd

    a = {k: np.asarray(v) for k, v in inputs.items()}
    x = a["x"][0]
    cols = lambda w: w.reshape(KD, P, -1, P).transpose(2, 1, 0, 3).reshape(-1, P, UN)
    conv_in = cols(a["a_w_in"][0]).reshape(3, KD, P, UN).transpose(1, 0, 2, 3).reshape(N_CONV, P, UN)
    w_dense0 = _pairs(np.concatenate([conv_in, a["a_w_out"][0].reshape(KD, P, UN)]))
    b_in = a["b_w_in"][0]
    blocks = lambda w: (w.reshape(w.shape[0] // (2 * P), 2, P, w.shape[1] // BANK, BANK)
                        .transpose(3, 0, 2, 1, 4).reshape(-1, P, UN))
    w_dense1 = _pairs(np.concatenate([cols(b_in[:, :SGU]), blocks(b_in[:, SGU:]), blocks(a["b_w_out"][0])]))
    gate_up = np.stack([a["moe_w_gate"], a["moe_w_up"]], axis=3)
    gate_up = gate_up.reshape(2, E, GU // 2, 2, P, UN)
    down = a["moe_w_down"].reshape(2, E, DN // 2, 2, P, UN)
    w_moe = np.concatenate([gate_up, down], axis=2).transpose(0, 1, 2, 4, 3, 5).reshape(2, E, EU // 2, P, 2 * UN)
    data = {
        "x": x,
        "x_t": x.T.reshape(4, 2, P, S).transpose(0, 2, 1, 3).reshape(4, P, 2 * S),
        "w_dense0": w_dense0,
        "w_moe": w_moe,
        "w_dense1": w_dense1,
        "conv_w": a["a_conv_w"][0].reshape(3, KD, P).transpose(2, 1, 0),
        "router_w": a["router_w"].reshape(KD, P, E).transpose(1, 0, 2),
        "router_bias": a["router_bias"],
        "w_s": a["b_ws"][0].transpose(1, 0, 2),
        "b_s": a["b_bs"][0].reshape(H * P),
        "v_gain": a["b_ln_g"][0].reshape(NC, P).T,
        "v_bias": a["b_ln_b"][0].reshape(NC, P).T,
        "ln_par": np.stack([np.stack([a["ln_mix_g"], a["ln_mix_b"]], 1), np.stack([a["ln_ffn_g"], a["ln_ffn_b"]], 1)], 1),
    }
    nc = bacc.Bacc("TRN2", target_bir_lowering=False, num_devices=1)
    arrays, args = {}, []
    for name, v in data.items():
        v = np.ascontiguousarray(v)
        arrays["in_" + name] = v
        args.append(nc.dram_tensor("in_" + name, v.shape, mybir.dt.from_np(v.dtype), kind="ExternalInput").ap())
    out = nc.dram_tensor("out", [S, D], F32, kind="ExternalOutput").ap()
    hybrid_decoder(nc, *args, out)
    r = run_bass_kernel_spmd(nc, [arrays], core_ids=[0])
    return r.results[0]["out"].reshape(1, S, D)
```
